# Optimizing a Trainium2 kernel written in Bass

```python
import math
import jax, jax.numpy as jnp
from jax import lax
import numpy as np

D_MODEL = 2048
BATCH = 1
SEQ = 512
DEPTH = 1
DEC_BATCH = 8
DEC_SEQ = 4
PAST_LEN = 4096
PAGE_SIZE = 128

S5_WIDTH = D_MODEL // 2
S5_GROUP = 16
S5_GROUPS = S5_WIDTH // S5_GROUP
S5_STATE = 64
DT_MIN = 1e-3
DT_MAX = 1e-1
POOL_WIDTH = D_MODEL // 2
POOL_WINDOWS = (2, 4, 8, 16)
POOL_GROUPS = len(POOL_WINDOWS)
POOL_GROUP_WIDTH = POOL_WIDTH // POOL_GROUPS
POOL_BUF = max(POOL_WINDOWS) - 1
IN_WIDTH = S5_WIDTH + POOL_WIDTH + 2 * D_MODEL
PEER_KEYS = 128
PEER_EXPERTS = PEER_KEYS * PEER_KEYS
PEER_HEADS = 8
PEER_QDIM = 256
PEER_HALF = PEER_QDIM // 2
PEER_TOPK = 16
PEER_BLOCK = 128
N_MOD = 6
EPS = 1e-6

kernel_name = "hybrid_s5_pool_peer_adaln_step"

def _rmsnorm(x, g):
    xf = x.astype(jnp.float32)
    return xf * lax.rsqrt(jnp.mean(xf * xf, axis=-1, keepdims=True) + EPS) * g.astype(jnp.float32)

def _s5_discretize(a_re, a_im, log_dt, b_re, b_im):
    a_re = a_re.astype(jnp.float32); a_im = a_im.astype(jnp.float32)
    dt = jnp.exp(log_dt.astype(jnp.float32))[:, None]
    lr, li = a_re * dt, a_im * dt
    mag = jnp.exp(lr)
    ab_re, ab_im = mag * jnp.cos(li), mag * jnp.sin(li)
    num_re, num_im = ab_re - 1.0, ab_im
    den = a_re * a_re + a_im * a_im
    f_re = (num_re * a_re + num_im * a_im) / den
    f_im = (num_im * a_re - num_re * a_im) / den
    b_re = b_re.astype(jnp.float32); b_im = b_im.astype(jnp.float32)
    bb_re = f_re[..., None] * b_re - f_im[..., None] * b_im
    bb_im = f_re[..., None] * b_im + f_im[..., None] * b_re
    return ab_re, ab_im, bb_re, bb_im

def _cplx_combine(e1, e2):
    a1r, a1i, b1r, b1i = e1
    a2r, a2i, b2r, b2i = e2
    return (a2r * a1r - a2i * a1i,
            a2r * a1i + a2i * a1r,
            a2r * b1r - a2i * b1i + b2r,
            a2r * b1i + a2i * b1r + b2i)

def _s5_branch(u, h0, a_re, a_im, log_dt, b_re, b_im, c_re, c_im, d_skip, w_glu, b_glu):
    bsz, t = u.shape[0], u.shape[1]
    ab_re, ab_im, bb_re, bb_im = _s5_discretize(a_re, a_im, log_dt, b_re, b_im)
    ug = u.reshape(bsz, t, S5_GROUPS, S5_GROUP)
    bu_re = jnp.einsum('btgc,gpc->btgp', ug, bb_re)
    bu_im = jnp.einsum('btgc,gpc->btgp', ug, bb_im)
    a_r = jnp.broadcast_to(ab_re, bu_re.shape)
    a_i = jnp.broadcast_to(ab_im, bu_re.shape)
    ap_re, ap_im, h_re, h_im = lax.associative_scan(_cplx_combine, (a_r, a_i, bu_re, bu_im), axis=1)
    if h0 is not None:
        h0_re = h0[0].astype(jnp.float32)[:, None]
        h0_im = h0[1].astype(jnp.float32)[:, None]
        h_re, h_im = (h_re + ap_re * h0_re - ap_im * h0_im,
                      h_im + ap_re * h0_im + ap_im * h0_re)
    y = (jnp.einsum('btgp,gcp->btgc', h_re, c_re.astype(jnp.float32))
         - jnp.einsum('btgp,gcp->btgc', h_im, c_im.astype(jnp.float32))).reshape(bsz, t, S5_WIDTH)
    y = y + d_skip.astype(jnp.float32) * u
    z = jax.nn.gelu(y, approximate=False)
    out = z * jax.nn.sigmoid(z @ w_glu + b_glu)
    return out, h_re[:, -1], h_im[:, -1]

def _pool_branch(u, buf, start_pos, w_pool, pool_scale):
    t = u.shape[1]
    ext = jnp.concatenate([buf.astype(jnp.float32), u], axis=1)
    cs = jnp.concatenate([jnp.zeros_like(ext[:, :1]), jnp.cumsum(ext, axis=1)], axis=1)
    end = cs[:, POOL_BUF + 1:]
    pos = start_pos + jnp.arange(t)
    outs = []
    for g, w in enumerate(POOL_WINDOWS):
        sl = slice(g * POOL_GROUP_WIDTH, (g + 1) * POOL_GROUP_WIDTH)
        cnt = jnp.minimum(pos + 1, w).astype(jnp.float32)[None, :, None]
        start = cs[:, POOL_BUF + 1 - w:POOL_BUF + 1 - w + t, sl]
        pooled = (end[..., sl] - start) / cnt - u[..., sl]
        outs.append(pooled @ w_pool[g])
    y = jnp.concatenate(outs, axis=-1) * pool_scale
    return y, ext[:, -POOL_BUF:]

def _peer(x, w_q, keys, u_tab, v_tab):
    bsz, t, d = x.shape
    xt = x.reshape(-1, d)
    n = xt.shape[0]
    xt = jnp.pad(xt, ((0, (-n) % PEER_BLOCK), (0, 0)))
    q = (xt @ w_q).reshape(-1, PEER_HEADS, 2, PEER_HALF)
    s = jnp.einsum('nhkd,hkmd->nhkm', q, keys).astype(jnp.float32)
    top_s, top_i = lax.top_k(s, PEER_TOPK)
    comb = (top_s[:, :, 0, :, None] + top_s[:, :, 1, None, :]).reshape(-1, PEER_HEADS, PEER_TOPK * PEER_TOPK)
    cidx = (top_i[:, :, 0, :, None] * PEER_KEYS + top_i[:, :, 1, None, :]).reshape(-1, PEER_HEADS, PEER_TOPK * PEER_TOPK)
    best_s, best_j = lax.top_k(comb, PEER_TOPK)
    expert = jnp.take_along_axis(cidx, best_j, axis=-1)
    gate = jax.nn.softmax(best_s, axis=-1)
    nb = xt.shape[0] // PEER_BLOCK
    xb = xt.reshape(nb, PEER_BLOCK, d)
    eb = expert.reshape(nb, PEER_BLOCK, PEER_HEADS * PEER_TOPK)
    gb = gate.reshape(nb, PEER_BLOCK, PEER_HEADS * PEER_TOPK)

    def block(args):
        xc, ec, gc = args
        act = jax.nn.gelu(jnp.einsum('nd,nkd->nk', xc, u_tab[ec]).astype(jnp.float32), approximate=False)
        return jnp.einsum('nk,nkd->nd', gc * act, v_tab[ec])

    out = lax.map(block, (xb, eb, gb)).reshape(-1, d)[:n]
    return out.reshape(bsz, t, d)

def _layer(x, c, h0, buf, start_pos, lw):
    (w_ada, b_ada, g1, g2, w_in, a_re, a_im, log_dt, b_re, b_im, c_re, c_im, d_skip,
     w_glu, b_glu, w_pool, pool_scale, p_a, p_b, w_o, w_q, keys, u_tab, v_tab) = lw
    mod = jax.nn.silu(c.astype(jnp.float32)) @ w_ada + b_ada
    sh1, sc1, gt1, sh2, sc2, gt2 = jnp.split(mod[:, None, :], N_MOD, axis=-1)
    h = _rmsnorm(x, g1) * (1.0 + sc1) + sh1
    z = h @ w_in
    u_a, u_b, z_ga, z_gb = jnp.split(z, [S5_WIDTH, S5_WIDTH + POOL_WIDTH, S5_WIDTH + POOL_WIDTH + D_MODEL], axis=-1)
    y_a, s_re, s_im = _s5_branch(u_a, h0, a_re, a_im, log_dt, b_re, b_im, c_re, c_im, d_skip, w_glu, b_glu)
    if buf is None:
        buf = jnp.zeros((u_b.shape[0], POOL_BUF, POOL_WIDTH), jnp.float32)
    y_b, new_buf = _pool_branch(u_b, buf, start_pos, w_pool, pool_scale)
    merged = jax.nn.sigmoid(z_ga) * (y_a @ p_a) + jax.nn.sigmoid(z_gb) * (y_b @ p_b)
    x = x + gt1 * (merged @ w_o)
    h2 = _rmsnorm(x, g2) * (1.0 + sc2) + sh2
    x = x + gt2 * _peer(h2, w_q, keys, u_tab, v_tab)
    return x, s_re, s_im, new_buf

def setup_inputs(seed: int = 0) -> dict:
    key = jax.random.key(seed)
    ks = iter(jax.random.split(key, 40))
    f32 = jnp.float32
    nrm = lambda shape, s: jax.random.normal(next(ks), shape, f32) * s
    inp = {}
    inp['x_prompt'] = nrm((BATCH, SEQ, D_MODEL), 1.0)
    inp['x_sample'] = nrm((DEC_BATCH, DEC_SEQ, D_MODEL), 1.0)
    inp['state_s5_re'] = nrm((DEPTH, DEC_BATCH, S5_GROUPS, S5_STATE), 0.5)
    inp['state_s5_im'] = nrm((DEPTH, DEC_BATCH, S5_GROUPS, S5_STATE), 0.5)
    inp['state_pool'] = nrm((DEPTH, DEC_BATCH, POOL_BUF, POOL_WIDTH), 1.0)
    inp['c_prompt'] = nrm((BATCH, D_MODEL), 1.0)
    inp['c_sample'] = nrm((DEC_BATCH, D_MODEL), 1.0)
    inp['w_ada'] = nrm((DEPTH, D_MODEL, N_MOD * D_MODEL), D_MODEL ** -0.5)
    inp['b_ada'] = nrm((DEPTH, N_MOD * D_MODEL), 0.01)
    inp['g_norm1'] = 1.0 + nrm((DEPTH, D_MODEL), 0.01)
    inp['g_norm2'] = 1.0 + nrm((DEPTH, D_MODEL), 0.01)
    inp['w_in'] = nrm((DEPTH, D_MODEL, IN_WIDTH), D_MODEL ** -0.5)
    inp['s5_a_re'] = -0.5 + nrm((DEPTH, S5_GROUPS, S5_STATE), 0.01)
    inp['s5_a_im'] = (math.pi * jnp.arange(S5_STATE, dtype=f32))[None, None, :] + nrm((DEPTH, S5_GROUPS, S5_STATE), 0.01)
    inp['s5_log_dt'] = jax.random.uniform(next(ks), (DEPTH, S5_GROUPS), f32, math.log(DT_MIN), math.log(DT_MAX))
    inp['s5_b_re'] = nrm((DEPTH, S5_GROUPS, S5_STATE, S5_GROUP), (2 * S5_GROUP) ** -0.5)
    inp['s5_b_im'] = nrm((DEPTH, S5_GROUPS, S5_STATE, S5_GROUP), (2 * S5_GROUP) ** -0.5)
    inp['s5_c_re'] = nrm((DEPTH, S5_GROUPS, S5_GROUP, S5_STATE), (2 * S5_STATE) ** -0.5)
    inp['s5_c_im'] = nrm((DEPTH, S5_GROUPS, S5_GROUP, S5_STATE), (2 * S5_STATE) ** -0.5)
    inp['s5_d'] = nrm((DEPTH, S5_WIDTH), 1.0)
    inp['w_glu'] = nrm((DEPTH, S5_WIDTH, S5_WIDTH), S5_WIDTH ** -0.5)
    inp['b_glu'] = nrm((DEPTH, S5_WIDTH), 0.01)
    inp['w_pool'] = nrm((DEPTH, POOL_GROUPS, POOL_GROUP_WIDTH, POOL_GROUP_WIDTH), POOL_GROUP_WIDTH ** -0.5)
    inp['pool_scale'] = 1.0 + nrm((DEPTH, POOL_WIDTH), 0.02)
    inp['w_proj_a'] = nrm((DEPTH, S5_WIDTH, D_MODEL), S5_WIDTH ** -0.5)
    inp['w_proj_b'] = nrm((DEPTH, POOL_WIDTH, D_MODEL), POOL_WIDTH ** -0.5)
    inp['w_out'] = nrm((DEPTH, D_MODEL, D_MODEL), D_MODEL ** -0.5)
    inp['peer_wq'] = nrm((DEPTH, D_MODEL, PEER_HEADS * PEER_QDIM), D_MODEL ** -0.5)
    inp['peer_keys'] = nrm((DEPTH, PEER_HEADS, 2, PEER_KEYS, PEER_HALF), PEER_HALF ** -0.5)
    inp['peer_u'] = nrm((DEPTH, PEER_EXPERTS, D_MODEL), D_MODEL ** -0.5)
    inp['peer_v'] = nrm((DEPTH, PEER_EXPERTS, D_MODEL), PEER_HEADS ** -0.5)
    inp['g_final'] = 1.0 + nrm((D_MODEL,), 0.01)
    return inp

def reference(x_prompt, x_sample, state_s5_re, state_s5_im, state_pool, c_prompt, c_sample,
              w_ada, b_ada, g_norm1, g_norm2, w_in, s5_a_re, s5_a_im, s5_log_dt, s5_b_re, s5_b_im,
              s5_c_re, s5_c_im, s5_d, w_glu, b_glu, w_pool, pool_scale, w_proj_a, w_proj_b, w_out,
              peer_wq, peer_keys, peer_u, peer_v, g_final):
    yp, ys = x_prompt, x_sample
    p_re, p_im, p_buf, s_re, s_im, s_buf = [], [], [], [], [], []
    for l in range(DEPTH):
        lw = (w_ada[l], b_ada[l], g_norm1[l], g_norm2[l], w_in[l], s5_a_re[l], s5_a_im[l], s5_log_dt[l],
              s5_b_re[l], s5_b_im[l], s5_c_re[l], s5_c_im[l], s5_d[l], w_glu[l], b_glu[l], w_pool[l],
              pool_scale[l], w_proj_a[l], w_proj_b[l], w_out[l], peer_wq[l], peer_keys[l], peer_u[l], peer_v[l])
        yp, r_re, r_im, r_buf = _layer(yp, c_prompt, None, None, 0, lw)
        ys, q_re, q_im, q_buf = _layer(ys, c_sample, (state_s5_re[l], state_s5_im[l]), state_pool[l], PAST_LEN, lw)
        p_re.append(r_re); p_im.append(r_im); p_buf.append(r_buf)
        s_re.append(q_re); s_im.append(q_im); s_buf.append(q_buf)
    y_prompt = _rmsnorm(yp, g_final).astype(x_prompt.dtype)
    y_sample = _rmsnorm(ys, g_final).astype(x_sample.dtype)
    return (y_prompt, y_sample,
            jnp.stack(p_re), jnp.stack(p_im), jnp.stack(p_buf),
            jnp.stack(s_re), jnp.stack(s_im), jnp.stack(s_buf))


_drawn_inputs = setup_inputs


def setup_inputs(seed=0):
    import zlib

    import numpy as np

    out = dict(_drawn_inputs(seed))
    spreads = {}
    factors = {'b_ada': 3.422,
     'g_norm1': 23.809,
     'g_norm2': 182.19,
     's5_a_re': 70.49,
     'b_glu': 200.0,
     'pool_scale': 13.504,
     'g_final': 196.123,
     's5_c_re': 36.721,
     's5_c_im': 22.289}
    for name, (base, spread) in spreads.items():
        noise = np.random.default_rng([zlib.crc32(name.encode()), seed]).standard_normal(out[name].shape)
        drawn = base * np.exp(spread * noise) if base else spread * noise
        out[name] = __import__('jax').numpy.asarray(drawn.astype(out[name].dtype))
    for name, factor in factors.items():
        out[name] = (out[name] * factor).astype(out[name].dtype)
    return out
```

```python
import math
from contextlib import ExitStack, contextmanager

import numpy as np
import concourse.bass as bass
from concourse import mybir

F32 = mybir.dt.float32
U32 = mybir.dt.uint32
ALU = mybir.AluOpType
ACT = mybir.ActivationFunctionType
AX = mybir.AxisListType

P = 128
D = 2048
KD = D // P
T = 512
SEQS, STEPS = 8, 4
NS = SEQS * STEPS
N = T + NS
HALF = N // 2
ROWT = T // P + 1
W = D // 2
KW = W // P
G, GC, ST = 64, 16, 64
L = 64
CHUNKS = T // L
NB, NA = 4, 8
BUF = 15
WINDOWS = (2, 4, 8, 16)
MODS = 6 * KD
SH1, SC1, GT1, SH2, SC2, GT2 = (KD * i for i in range(6))
C9 = 1 + SEQS
HEADS, TOPK = 8, 16
SLOTS = HEADS * TOPK
EPS = 1e-6
LOW = -3.0e38
TWO_PI = (6.28125, 1.9350051879882812e-3, 3.019916e-7)
ROUND = 12582912.0

SLAB = 2048
RING = 0
HT = RING + 4 * SLAB
MG = HT + KD * N
UA = MG + KD * N
UB = UA + KW * N
E = UB + KW * N
BB = E + 7168
CT = BB + 2048
US = CT + 2048
PH = US + 512
MOD = PH + 4096
CON = MOD + MODS * C9
NCON = 128 + 16 + 64 + 32 + 1
BT = CON + NCON
VT = BT + MODS
CS = VT + 56
AB = CS + KD * C9
CR = AB + 64
HL = CR + 64
H0 = HL + 64
SS = H0 + 512
ARENA = SS + 64

X1 = UA
XN = X1 + ROWT * D
KT = PH
IX = PH + 2048
GT = IX + ROWT * SLOTS
TS = GT + ROWT * SLOTS
TI = TS + ROWT * 32
BJ = TI + ROWT * 32

S5_PAIR = 4 + 4 + KD
WQ_PAIR = S5_PAIR + 4 * (CHUNKS + 1) + 1 + 2 + 1 + 3 * KD + 2

SEMS = """consts_in c_in vec_in s5par_in h0_in c_zeroed c_weights_in b_weights_in x_in wpool_in pool_in keys_in
gfinal_in silu_done pair_full pair_free product_done acc_free ada_free staged h_ready y_done y_free act_step
dve_step dve_to_act act_to_dve mods_ready col_ready ua_ready ub_ready bb_ready s5_done y_ready z_ready
glu_ready pooled yb_ready ya_ready piece_done merged_ready out_ready rows_laid state_rows state_out x1_ready
idx_ready idx_staged u_used v_used act_ready gelu_ready w_ready diag_ready peer_free fin_in fin_sum fin_row
fin_out keys_laid expand_ready xn_ready dve_stood pool_stood""".split()


class Count:

    def __init__(self, start=0):
        self.n, self.i, self.per = start, None, 0

    def step(self, k=1):
        self.n += k
        return self.value()

    def value(self):
        return self.n if self.i is None else self.n + self.i * self.per


class Own:

    def __init__(self, eng, sem, start=0):
        self.eng, self.sem, self.count = eng, sem, Count(start)

    def did(self, instruction):
        instruction.then_inc(self.sem, 1)
        self.count.step()

    def settle(self):
        self.eng.wait_ge(self.sem, self.count.value())

    def then(self, instruction):
        self.did(instruction)
        self.settle()


@contextmanager
def loop(eng, times, *counts):
    starts = [c.n for c, _ in counts]
    with eng.Fori(0, times) as i:
        for c, per in counts:
            c.i, c.per = i, per
        yield i
    for k, ((c, per), n) in enumerate(zip(counts, starts)):
        assert c.n - n == per, (k, c.n - n, per)
        c.n, c.i = n + per * times, None


def bc(ap, axis, count):
    ap = ap.unsqueeze(axis)
    shape = list(ap.shape)
    shape[axis] = count
    return ap.to_broadcast(shape)


def at(start, n):
    return bass.ds(start, n)


def layer(nc, i_, o_):
    with ExitStack() as ctx:
        A = ctx.enter_context(nc.sbuf_tensor("arena", [P, ARENA], F32))
        ps = ctx.enter_context(nc.psum_tensor("banks", [P, 4096], F32))
        s = {n: ctx.enter_context(nc.semaphore(n)) for n in SEMS}
        ring_full = [ctx.enter_context(nc.semaphore(f"ring_full{j}")) for j in range(4)]
        u_full = [ctx.enter_context(nc.semaphore(f"u_full{j}")) for j in range(4)]
        v_full = [ctx.enter_context(nc.semaphore(f"v_full{j}")) for j in range(4)]

        def V(off, n):
            return A[:, off:off + n]

        def V3(off, a, b):
            return V(off, a * b).rearrange("p (a b) -> p a b", a=a)

        def V4(off, a, b, c):
            return V(off, a * b * c).rearrange("p (a b c) -> p a b c", a=a, b=b)

        ident, iota16, corr = V(CON, 128), V(CON + 128, 16), V3(CON + 144, 4, 16)
        fold, half_pi = V(CON + 208, 32), V(CON + 240, 1)
        vecs = V(VT, 56)
        g1T, g2T = vecs[:, 0:16], vecs[:, 16:32]
        bgluT, pscaleT, dT = vecs[:, 32:40], vecs[:, 40:48], vecs[:, 48:56]
        mod = V3(MOD, MODS, C9)
        cT = V3(CS, KD, C9)
        ss, rstd = V(SS, ROWT), V(SS + 8, ROWT)
        bank = [ps[:, 512 * j:512 * j + 512] for j in range(8)]
        ACC, ADA, YB = (bank[0], bank[1]), bank[2], bank[7]
        PAIR = ((bank[3], bank[4]), (bank[5], bank[6]))
        slab16 = [V3(RING + SLAB * j, 16, 128) for j in range(4)]
        slab8 = [V3(RING + SLAB * j, 8, 256) for j in range(4)]
        hT, mT, uaT, ubT = V3(HT, KD, N), V3(MG, KD, N), V3(UA, KW, N), V3(UB, KW, N)
        ybT, yaT, wpool = V3(E, KW, N), V3(BB, KW, N), V3(E + KW * N, 8, 256)
        tabc, tabs, coef = V4(E, NB, NA, L), V4(E + 2048, NB, NA, L), V4(E + 4096, NB, NA, L)
        coefS = V(E + 6144, 1024)
        BBT = (V3(BB, NA, 128), V3(BB + 1024, NA, 128))
        CTT = (V3(CT, NA, 128), V3(CT + 1024, NA, 128))
        ustage = V3(US, NA, L)
        W1, W2, W3, W4 = (V(PH + 512 * j, 512) for j in range(4))
        HB = [(V(PH + 2048 + 1024 * j, 512), V(PH + 2560 + 1024 * j, 512)) for j in range(2)]
        abr, abi, crr, cri, hlr, hli = (V(AB + 32 * j, 32) for j in range(6))
        h0 = (V(H0, 256), V(H0 + 256, 256))
        c_rows, vec_rows, par_rows = MG, MG + D, MG + D + 256
        h0_rows = (V3(MG + 2816, 2, 128), V3(MG + 3072, 2, 128))
        c_wide = (V3(MG + 3328, NA, 128), V3(MG + 4352, NA, 128))
        b_nat = (V3(MG + 5376, 32, GC), V3(MG + 5888, 32, GC))
        b_wide = (V3(MG + 6400, 32, 32), V3(MG + 7424, 32, 32))
        x1, xn = V3(X1, ROWT, D), V3(XN, ROWT, D)
        out_prompt_rows, out_sample_rows = V(PH + 1024, 1024), V(PH + 2048, 1024)
        piece = (V(PH, HALF), V(PH + HALF, HALF))
        sig = [V(PH + (2 + j) * HALF, HALF) for j in range(4)]
        keysT, keys_nat = V3(KT, 16, 128), V3(HT + 3648, 16, 128)
        ix, gates = V(IX, ROWT * SLOTS).bitcast(U32), V(GT, ROWT * SLOTS)
        qT = (V(HT, 544 + 96), V(HT + 640, 640))
        ubuf = [V(RING + D * j, D) for j in range(4)]
        vbuf = [V(HT + D * j, D) for j in range(4)]
        gfin, gt2P, gt2S, fin = (V(MG + D * j, D) for j in range(4))
        acts, wts = ([V(KT + 256 * q + 128 * j, 128) for j in range(2)] for q in range(2))
        diag = [V(KT + 512 + 128 * j, 128) for j in range(4)]
        ixS, gS = V(KT + 1024, 32).bitcast(U32), V(KT + 1056, 32)
        uix, vix = V(KT + 1088, 4).bitcast(U32), V(KT + 1092, 4).bitcast(U32)
        psum4 = [ps[:, 0:2048], ps[:, 2048:4096]]

        block = ctx.enter_context(nc.Block())

        @block.sync
        def _(sp):
            def blocks(name):
                return i_[name].rearrange("(k p) n -> p k n", p=P)

            w_in, w_ada, w_out, w_q = (blocks(n) for n in ("w_in", "w_ada", "w_out", "peer_wq"))
            w_glu, w_pa, w_pb = (blocks(n) for n in ("w_glu", "w_proj_a", "w_proj_b"))
            history = [None] * 4

            def load_rows():
                sp.dma_start(x1[:, 0:4, :], i_["x_prompt"].rearrange("b (t p) d -> (b p) t d", p=P)
                             ).then_inc(s["x_in"], 16)
                for r in range(4):
                    sp.dma_start(A[32 * r:32 * r + 32, X1 + 4 * D:X1 + 5 * D],
                                 i_["x_sample"].rearrange("s t d -> (s t) d")).then_inc(s["x_in"], 16)

            def laps(times, slots, base):
                total = sum(x[4] for x in slots)
                read = [sum(x[4] for x in slots[:j + 1]) for j in range(4)]

                def one(i, finished):
                    for j, (w, cols, m0, step, _) in enumerate(slots):
                        if finished[j] is not None:
                            sp.wait_ge(s["product_done"], finished[j])
                        sp.dma_start((slab16 if cols == 128 else slab8)[j],
                                     w[:, :, at((i * step + m0) * cols, cols)]).then_inc(ring_full[j], 16)

                one(0, history)
                if times > 1:
                    with sp.Fori(1, times) as i:
                        one(i, [i * total + (base - total + read[j]) for j in range(4)])
                for j in range(4):
                    history[j] = base + (times - 1) * total + read[j]
                return base + times * total

            def pairs(w, m0, mods, cols=128, products=2):
                return [(w, cols, m0, 2, products), (w_ada, 128, mods, 2, 1),
                        (w, cols, m0 + 1, 2, products), (w_ada, 128, mods + 1, 2, 1)]

            load_rows()
            b = laps(8, [(w_ada, 128, j, 4, 1) for j in range(4)], 0)
            b = laps(4, pairs(w_in, 0, GT1), b)
            b = laps(4, pairs(w_in, 8, GT1 + 8), b)
            b = laps(8, pairs(w_in, 32, SH2), b)
            b = laps(1, [(w_glu, 256, j, 4, 4) for j in range(4)], b)
            sp.wait_ge(s["s5_done"], 1)
            sp.dma_start(A[0:SEQS * BUF, E:E + W], i_["state_pool"].rearrange("s r c -> (s r) c")
                         ).then_inc(s["pool_in"], 16)
            sp.dma_start(wpool, i_["w_pool"].rearrange("g (k p) n -> p (g k) n", p=P)).then_inc(s["wpool_in"], 16)
            b += 2 * KW
            b = laps(4, pairs(w_pb, 0, SC2, 256, 4), b)
            b = laps(8, [(w_in, 128, 16, 2, 2), (w_ada, 128, SC2 + 8, 1, 1),
                         (w_in, 128, 17, 2, 2), (w_pa, 256, 0, 1, 4)], b)
            b = laps(1, pairs(w_out, 0, GT2), b)
            sp.wait_ge(s["merged_ready"], 1)
            load_rows()
            b = laps(7, pairs(w_out, 2, GT2 + 2), b)
            b = laps(4, [(w_q, 128, j, 4, 2) for j in range(4)], b)
            for t in range(ROWT):
                sp.wait_ge(s["fin_row"], t + 1)
                if t < 4:
                    sp.dma_start(o_["y_prompt"].rearrange("b (t p) d -> (b p) t d", p=P)[:, t, :], x1[:, t, :]
                                 ).then_inc(s["fin_out"], 16)
                else:
                    sp.dma_start(o_["y_sample"].rearrange("s t d -> (s t) d"), A[0:NS, X1 + 4 * D:X1 + 5 * D]
                                 ).then_inc(s["fin_out"], 16)
            sp.wait_ge(s["fin_out"], 16 * ROWT)

        @block.gpsimd
        def _(pool):
            dma = pool.dma_start
            dma(V(CON, NCON), i_["consts"]).then_inc(s["consts_in"], 16)
            dma(A[0:1, c_rows:c_rows + D], i_["c_prompt"]).then_inc(s["c_in"], 16)
            dma(A[1:C9, c_rows:c_rows + D], i_["c_sample"]).then_inc(s["c_in"], 16)
            dma(A[0:MODS, vec_rows:vec_rows + 128], i_["b_ada"].rearrange("(m q) -> m q", q=P)
                ).then_inc(s["vec_in"], 16)
            r = 0
            for name, rows in (("g_norm1", KD), ("g_norm2", KD), ("b_glu", KW), ("pool_scale", KW), ("s5_d", KW)):
                dma(A[r:r + rows, vec_rows + 128:vec_rows + 256], i_[name].rearrange("(m q) -> m q", q=P)
                    ).then_inc(s["vec_in"], 16)
                r += rows
            for k, name in enumerate(("s5_a_re", "s5_a_im")):
                dma(A[0:32, par_rows + 128 * k:par_rows + 128 * k + 128],
                    i_[name].rearrange("(i g) q -> i (g q)", g=2)).then_inc(s["s5par_in"], 16)
            dma(A[0:32, par_rows + 384:par_rows + 386], i_["s5_log_dt"].rearrange("(i g) -> i g", g=2)
                ).then_inc(s["s5par_in"], 16)
            for k, name in enumerate(("state_s5_re", "state_s5_im")):
                rows = i_[name].rearrange("(u s) (i g) q -> u (s i) (g q)", u=2, g=2)
                for u in range(2):
                    dma(h0_rows[k][:, u, :], rows[u]).then_inc(s["h0_in"], 16)
            for k, name in enumerate(("s5_b_re", "s5_b_im")):
                dma(b_nat[k], i_[name].rearrange("(i g) q c -> (g q) i c", g=2)).then_inc(s["b_weights_in"], 16)
            pool.wait_ge(s["c_zeroed"], 1)
            for k, name in enumerate(("s5_c_re", "s5_c_im")):
                src = i_[name].rearrange("(a b g) c q -> b g c a q", b=NB, g=2)
                for b in range(NB):
                    for g in range(2):
                        r = 32 * b + 16 * g
                        dma(c_wide[k][r:r + 16, :, 64 * g:64 * g + 64], src[b, g]).then_inc(s["c_weights_in"], 16)
            dma(o_["new_pool_sample"][:, 0:BUF - STEPS, :], i_["state_pool"][:, STEPS:BUF, :]
                ).then_inc(s["state_out"], 16)
            pool.wait_ge(s["state_rows"], 1)
            for k, name in enumerate(("new_s5_re_prompt", "new_s5_im_prompt")):
                dma(o_[name].rearrange("(i g) q -> i (g q)", g=2), A[0:32, PH + 128 * k:PH + 128 * k + 128]
                    ).then_inc(s["state_out"], 16)
            for k, name in enumerate(("new_s5_re_sample", "new_s5_im_sample")):
                rows = o_[name].rearrange("(u s) (i g) q -> u (s i) (g q)", u=2, g=2)
                for u in range(2):
                    dma(rows[u], V(PH + 256 + 256 * k + 128 * u, 128)).then_inc(s["state_out"], 16)
            dma(o_["new_pool_prompt"], out_prompt_rows[0:BUF, :]).then_inc(s["state_out"], 16)
            for q in range(SEQS):
                dma(o_["new_pool_sample"][q, BUF - STEPS:BUF, :],
                    out_sample_rows[STEPS * q:STEPS * q + STEPS, :]).then_inc(s["state_out"], 16)
            pool.wait_ge(s["state_out"], 16 * 16)
            pool.wait_ge(s["x1_ready"], 1)
            dma(keys_nat, i_["peer_keys"].rearrange("h k m d -> m (h k) d")).then_inc(s["keys_in"], 16)

            staged, used = Count(), {"u": Count(), "v": Count()}
            side = {"u": (i_["peer_u"], ubuf, uix, u_full, s["u_used"]),
                    "v": (i_["peer_v"], vbuf, vix, v_full, s["v_used"])}

            def gather(kind, r, column):
                table, buf, stage, full, freed = side[kind]
                pool.wait_ge(freed, used[kind].step())
                nc.gpsimd.tensor_copy(stage[:, r:r + 1], column).then_inc(s["idx_staged"], 1)
                pool.wait_ge(s["idx_staged"], staged.step())
                pool.sem_inc(s["pool_stood"], 1)
                nc.gpsimd.indirect_dma_start(
                    buf[r], None, table, bass.IndirectOffsetOnAxis(ap=stage[:, r:r + 1], axis=0),
                ).then_inc(full[r], 16)

            pool.wait_ge(s["idx_ready"], 1)
            dma(gfin, i_["g_final"].partition_broadcast(P)).then_inc(s["gfinal_in"], 16)
            with loop(pool, 32, (staged, 4), (used["u"], 4)) as i:
                for r in range(4):
                    gather("u", r, ix[:, at(i * 4 + r, 1)])
            with loop(pool, 96, (staged, 8), (used["u"], 4), (used["v"], 4)) as i:
                for r in range(4):
                    gather("u", r, ix[:, at(i * 4 + (128 + r), 1)])
                    gather("v", r, ix[:, at(i * 4 + r, 1)])
            with loop(pool, 8, (staged, 20), (used["u"], 4), (used["v"], 16)) as i:
                for r in range(4):
                    gather("u", r, ixS[:, at(i * 4 + r, 1)])
                    for q in range(4):
                        gather("v", q, ix[:, at(i * 16 + (384 + 4 * r + q), 1)])
            with loop(pool, 8, (staged, 4), (used["v"], 4)) as i:
                for r in range(4):
                    gather("v", r, ixS[:, at(i * 4 + r, 1)])

        @block.tensor
        def _(pe):
            mm = nc.tensor.matmul
            pairs, lap = Count(), Count()
            acc, ada_, h_in, yfree = Count(), Count(), Count(), Count()
            pe.sem_inc(s["y_done"], 2)
            pe.sem_inc(s["v_used"], 4)

            def turn(items):
                pe.wait_ge(s["pair_free"], pairs.step())
                for out, in_ in items:
                    last = nc.tensor.transpose(out, in_, ident[0:in_.shape[0], 0:in_.shape[0]])
                last.then_inc(s["pair_full"], 1)

            def pair():
                return PAIR[pairs.n % 2]

            def arrived(j):
                pe.wait_ge(ring_full[j], lap.value() * 16 + 16)

            def product(weights, src, blocks, halves=(0, 1)):
                for h in halves:
                    pe.wait_ge(s["acc_free"], acc.step())
                    for n, (w, k) in enumerate(zip(weights, blocks)):
                        last = mm(ACC[h][:, 0:HALF], w, src[:, k, HALF * h:HALF * h + HALF],
                                  start=n == 0, stop=n == len(blocks) - 1)
                    last.then_inc(s["product_done"], 1)

            def main16(j, src, halves=(0, 1)):
                if 0 in halves:
                    arrived(j)
                product([slab16[j][:, k, :] for k in range(16)], src, range(16), halves)

            def main8(j, src):
                arrived(j)
                for m in range(2):
                    product([slab8[j][:, k, 128 * m:128 * m + 128] for k in range(8)], src, range(8))

            def ada(j):
                arrived(j)
                pe.wait_ge(s["ada_free"], ada_.step())
                for k in range(KD):
                    last = mm(ADA[:, 0:C9], slab16[j][:, k, :], cT[:, k, :], start=k == 0, stop=k == KD - 1)
                last.then_inc(s["product_done"], 1)

            pe.wait_ge(s["consts_in"], 16)
            pe.wait_ge(s["silu_done"], 1)
            X, Z = pair()
            turn([(X[:, C9 * k:C9 * k + C9], A[0:C9, c_rows + 128 * k:c_rows + 128 * k + 128]) for k in range(KD)])
            pe.wait_ge(s["vec_in"], 96)
            X, Z = pair()
            turn([(X[:, 0:MODS], A[0:MODS, vec_rows:vec_rows + 128]),
                  (Z[:, 0:56], A[0:56, vec_rows + 128:vec_rows + 256])])
            pe.wait_ge(s["rows_laid"], 1)
            X, Z = pair()
            turn([(X[:, 32 * k:32 * k + 32], A[0:32, par_rows + 128 * k:par_rows + 128 * k + 128])
                  for k in range(3)])
            pe.wait_ge(s["h0_in"], 64)
            X, Z = pair()
            turn([((X, Z)[k][:, 128 * u:128 * u + 128], h0_rows[k][:, u, :]) for k in range(2) for u in range(2)])
            pe.wait_ge(s["col_ready"], 1)
            with loop(pe, 8, (lap, 1), (ada_, 4)):
                for j in range(4):
                    ada(j)
                lap.step()
            pe.wait_ge(s["c_weights_in"], 16 * 16)
            for k in range(2):
                X, Z = pair()
                turn([((X, Z)[a // 4][:, 128 * (a % 4):128 * (a % 4) + 128], c_wide[k][:, a, :]) for a in range(NA)])
            pe.wait_ge(s["bb_ready"], 1)
            for k in range(2):
                X, Z = pair()
                turn([((X, Z)[a // 4][:, 128 * (a % 4):128 * (a % 4) + 128],
                       b_wide[k][:, 4 * a:4 * a + 4, :].rearrange("p a b -> p (a b)")) for a in range(NA)])

            def rows_to_columns(src):
                for k in range(KD):
                    X, Z = pair()
                    turn([(X[:, 128 * t:128 * t + 128] if t < 4 else Z[:, 0:128],
                           src[:, t, 128 * k:128 * k + 128]) for t in range(ROWT)])

            def columns_to_rows(src, wide):
                for k in range(KD):
                    X, Z = pair()
                    turn([(X[:, 128 * t:128 * t + 128], src[:, k, 128 * t:128 * t + 128]) for t in range(4)]
                         + [(Z[:, 0:128], wide[:, k, :])])

            pe.wait_ge(s["xn_ready"], 1)
            rows_to_columns(x1)
            pe.wait_ge(s["col_ready"], 2)
            for _ in range(2):
                with loop(pe, 4, (lap, 1), (acc, 4), (ada_, 2)):
                    for j in (0, 2):
                        main16(j, hT)
                        ada(j + 1)
                    lap.step()

            def s5_in(b, n):
                X, Z = pair()
                pe.wait_ge(s["pair_free"], pairs.step())
                for k, out in enumerate((X, Z)):
                    for a in range(NA):
                        last = mm(out[:, n * a:n * a + n], BBT[k][32 * b:32 * b + 32, a, :],
                                  ustage[32 * b:32 * b + 32, a, 0:n], start=True, stop=True)
                last.then_inc(s["pair_full"], 1)

            def s5_out(b, n):
                pe.wait_ge(s["h_ready"], h_in.step())
                if b == 0:
                    pe.wait_ge(s["y_free"], yfree.step())
                hr, hi = HB[b % 2]
                for a in range(NA):
                    out = YB[32 * b:32 * b + 32, n * a:n * a + n]
                    mm(out, CTT[0][:, a, 32 * b:32 * b + 32], hr[:, n * a:n * a + n], start=True, stop=False)
                    last = mm(out, CTT[1][:, a, 32 * b:32 * b + 32], hi[:, n * a:n * a + n], start=False, stop=True)
                last.then_inc(s["y_done"], 1)

            stages = Count()

            def chunk(after):
                for b in range(NB):
                    if b < NB - 1:
                        s5_in(b + 1, L)
                    else:
                        pe.wait_ge(s["staged"], stages.step())
                        s5_in(0, after)
                    main16(2 * (b // 2), hT, (b % 2,))
                    if b % 2:
                        ada(2 * (b // 2) + 1)
                    s5_out(b, L)
                lap.step()

            pe.wait_ge(s["staged"], stages.step())
            s5_in(0, L)
            with loop(pe, CHUNKS - 1, (lap, 1), (acc, 4), (ada_, 2), (pairs, 4), (h_in, 4), (yfree, 1), (stages, 1)):
                chunk(L)
            chunk(NS)
            for b in range(NB):
                if b < NB - 1:
                    s5_in(b + 1, NS)
                s5_out(b, NS)
            pe.wait_ge(s["rows_laid"], 2)
            X, Z = pair()
            turn([(X[0:32, 128 * k:128 * k + 128], V(PH + 3072 + 32 * k, 32)) for k in range(2)]
                 + [(Z[:, 128 * k:128 * k + 128], V(PH + 3136 + 128 * k, 128)) for k in range(4)])
            pe.wait_ge(s["ub_ready"], 1)
            for c0, n in ((T - BUF, BUF), (T, NS)):
                X, Z = pair()
                turn([((X, Z)[a // 4][0:n, 128 * (a % 4):128 * (a % 4) + 128], ubT[:, a, c0:c0 + n])
                      for a in range(NA)])
            pe.wait_ge(s["z_ready"], 1)
            for j in range(4):
                main8(j, uaT)
            lap.step()
            pe.wait_ge(s["pool_in"], 16)
            X, Z = pair()
            turn([((X, Z)[a // 4][:, 120 * (a % 4):120 * (a % 4) + 120],
                   A[0:SEQS * BUF, E + 128 * a:E + 128 * a + 128]) for a in range(NA)])
            pe.wait_ge(s["wpool_in"], 16)
            pe.wait_ge(s["pooled"], 1)
            for g in range(4):
                for m in range(2):
                    product([wpool[:, 2 * g + k, 128 * m:128 * m + 128] for k in range(2)], ubT,
                            (2 * g, 2 * g + 1))
            pe.wait_ge(s["yb_ready"], 1)
            with loop(pe, 4, (lap, 1), (acc, 8), (ada_, 2)):
                for j in (0, 2):
                    main8(j, ybT)
                    ada(j + 1)
                lap.step()
            pe.wait_ge(s["ya_ready"], 1)
            with loop(pe, 8, (lap, 1), (acc, 8), (ada_, 1)):
                main16(0, hT)
                ada(1)
                main16(2, hT)
                main8(3, yaT)
                lap.step()
            pe.wait_ge(s["merged_ready"], 1)
            with loop(pe, 8, (lap, 1), (acc, 4), (ada_, 2)):
                for j in (0, 2):
                    main16(j, mT)
                    ada(j + 1)
                lap.step()
            pe.wait_ge(s["expand_ready"], 1)
            columns_to_rows(hT, V3(MG, KD, 128))
            pe.wait_ge(s["xn_ready"], 2)
            rows_to_columns(xn)
            pe.wait_ge(s["expand_ready"], 2)
            columns_to_rows(mT, V3(HT, KD, 128))
            pe.wait_ge(s["keys_in"], 16)
            for half in range(2):
                X, Z = pair()
                turn([((X, Z)[k // 4][:, 128 * (k % 4):128 * (k % 4) + 128], keys_nat[:, 8 * half + k, :])
                      for k in range(8)])
            pe.wait_ge(s["keys_laid"], 1)
            with loop(pe, 4, (lap, 1), (acc, 8), (pairs, 4)) as i:
                for j in range(4):
                    main16(j, mT)
                    X, Z = pair()
                    pe.wait_ge(s["pair_free"], pairs.step())
                    pe.wait_ge(s["acc_free"], acc.value() + 2)
                    for t in range(ROWT):
                        last = mm(X[:, 128 * t:128 * t + 128] if t < 4 else Z[:, 0:128],
                                  qT[j % 2][:, 128 * t:128 * t + 128],
                                  V(KT, 2048)[:, at((i * 4 + j) * 128, 128)], start=True, stop=True)
                    last.then_inc(s["pair_full"], 1)
                lap.step()
            pe.wait_ge(s["expand_ready"], 3)
            for q, rows in ((0, 128), (1, 128), (0, NS), (1, NS)):
                X, Z = pair()
                off = HT + (0 if rows == 128 else 2048)
                turn([((X, Z)[k // 4][0:rows, 128 * (k % 4):128 * (k % 4) + 128],
                       V(off + rows * (8 * q + k), rows)) for k in range(8)])

            vlap, dg = Count(), Count()
            for t in range(ROWT):
                rows = 128 if t < 4 else NS
                acc4 = psum4[t % 2]
                pe.wait_ge(s["peer_free"], t + 1)

                def slots(first, last_):
                    for r in range(4):
                        pe.wait_ge(s["diag_ready"], dg.step())
                        pe.wait_ge(v_full[r], vlap.value() * 16 + 16)
                        for n in range(4):
                            last = mm(acc4[0:rows, 512 * n:512 * n + 512], diag[r][:, 0:rows],
                                      vbuf[r][:, 512 * n:512 * n + 512],
                                      start=first and r == 0, stop=last_ and r == 3)
                        last.then_inc(s["v_used"], 1)
                    vlap.step()

                slots(True, False)
                with loop(pe, (32 if t < 4 else 8) - 2, (vlap, 1), (dg, 4)):
                    slots(False, False)
                slots(False, True)

        @block.scalar
        def _(act):
            fn = nc.scalar.activation
            product, acc, adas, pairs = Count(), Count(2), Count(1), Count()
            from_dve, pieces = Count(), Count()
            own = Own(act, s["act_step"])
            act.sem_inc(s["acc_free"], 2)
            act.sem_inc(s["ada_free"], 1)

            def read(h, out, func, free=True, **kw):
                act.wait_ge(s["product_done"], product.step())
                fn(out, ACC[h][:, 0:HALF], func, **kw).then_inc(s["acc_free"], 1)
                acc.step()

            def ada(m):
                act.wait_ge(s["product_done"], product.step())
                fn(A[:, at(MOD + m * C9, C9)], ADA[:, 0:C9], ACT.Identity, bias=A[:, at(BT + m, 1)]
                   ).then_inc(s["ada_free"], 1)
                adas.step()

            def block_of(base, m):
                return [A[:, at(base + m * N + HALF * h, HALF)] for h in range(2)]

            def done(name, k=1):
                act.wait_ge(s["acc_free"], acc.value())
                act.sem_inc(s[name], k)

            def row_norms(src, junk):
                for t in range(ROWT):
                    own.then(fn(junk, src[:, t, :], ACT.Square, accum_out=ss[:, t:t + 1]))
                act.sem_inc(s["act_to_dve"], 1)
                act.wait_ge(s["dve_to_act"], from_dve.step())
                fn(rstd, rstd, ACT.Sqrt).then_inc(s["act_to_dve"], 1)

            act.wait_ge(s["c_in"], 32)
            cr = A[0:C9, c_rows:c_rows + D]
            fn(cr, cr, ACT.Silu).then_inc(s["silu_done"], 1)
            dt, lr, ph, phabs = (V(PH + 64 + 32 * j, 32) for j in range(4))
            act.wait_ge(s["dve_to_act"], from_dve.step())
            fn(dt, dt, ACT.Exp).then_inc(s["act_to_dve"], 1)
            act.wait_ge(s["dve_to_act"], from_dve.step())
            fn(lr, lr, ACT.Exp)
            fn(ph, ph, ACT.Sin)
            act.wait_ge(s["consts_in"], 16)
            fn(phabs, phabs, ACT.Sin, scale=-1.0, bias=half_pi).then_inc(s["act_to_dve"], 1)
            act.wait_ge(s["x_in"], 80)
            row_norms(x1, V(HT, D))
            act.wait_ge(s["mods_ready"], 1)
            with loop(act, 8, (product, 4), (adas, 4)) as i:
                for j in range(4):
                    ada(i * 4 + j)
            act.wait_ge(s["ada_free"], adas.value())
            act.sem_inc(s["mods_ready"], 1)
            for base, m0, name in ((UA, 0, "ua_ready"), (UB, 8, "ub_ready")):
                with loop(act, 4, (product, 6), (acc, 4), (adas, 2)) as i:
                    for j in range(2):
                        for h in range(2):
                            read(h, block_of(base, i * 2 + j)[h], ACT.Copy)
                        ada(i * 2 + (GT1 + m0 + j))
                done(name)
                if name == "ua_ready":
                    fn(ustage, uaT[:, :, 0:L], ACT.Copy).then_inc(s["staged"], 1)
            pairs.n = S5_PAIR

            def chunk(c, last):
                for b in range(NB):
                    read(b % 2, block_of(MG, c * 2 + b // 2)[b % 2], ACT.Sigmoid)
                    if b % 2:
                        ada(c * 2 + (SH2 + b // 2))
                    if b == 2:
                        act.wait_ge(s["pair_full"], pairs.step(4))
                        if last:
                            fn(ustage[:, :, 0:NS], uaT[:, :, T:N], ACT.Copy).then_inc(s["staged"], 1)
                        else:
                            src = V(UA, KW * N).rearrange("p (a n) -> p a n", a=KW)
                            fn(ustage, src[:, :, at(c * L + L, L)], ACT.Copy).then_inc(s["staged"], 1)

            with loop(act, CHUNKS - 1, (product, 6), (acc, 4), (adas, 2), (pairs, 4)) as c:
                chunk(c, False)
            chunk(CHUNKS - 1, True)
            act.wait_ge(s["y_ready"], 1)
            fn(V(UA, KW * N), V(UA, KW * N), ACT.Gelu).then_inc(s["z_ready"], 1)
            for m in range(KW):
                for h in range(2):
                    read(h, yaT[:, m, HALF * h:HALF * h + HALF], ACT.Sigmoid, bias=bgluT[:, m:m + 1])
            done("glu_ready")
            for m in range(KW):
                for h in range(2):
                    read(h, ybT[:, m, HALF * h:HALF * h + HALF], ACT.Copy, scale=pscaleT[:, m:m + 1])
            done("yb_ready")

            def piece_out(h):
                act.wait_ge(s["piece_done"], pieces.step())
                read(h, piece[h], ACT.Copy)

            with loop(act, 4, (product, 10), (acc, 8), (adas, 2), (pieces, 8)) as i:
                for j in range(2):
                    for _ in range(2):
                        for h in range(2):
                            piece_out(h)
                    ada(i * 2 + (SC2 + j))
            with loop(act, 8, (product, 9), (acc, 8), (adas, 1), (pieces, 4)) as i:
                act.wait_ge(s["piece_done"], pieces.value() + 2)
                for j in range(2):
                    for h in range(2):
                        read(h, sig[2 * j + h], ACT.Sigmoid)
                    if j == 0:
                        ada(i + (SC2 + 8))
                for _ in range(2):
                    for h in range(2):
                        piece_out(h)
            act.wait_ge(s["ada_free"], adas.value())
            with loop(act, 8, (product, 6), (acc, 4), (adas, 2)) as i:
                for j in range(2):
                    m = i * 2 + j
                    gate = A[:, at(m * C9 + (MOD + GT1 * C9), 1)]
                    read(0, A[:, at(m * N + HT, HALF)], ACT.Copy, scale=gate)
                    act.wait_ge(s["product_done"], product.step())
                    fn(A[:, at(m * N + (HT + HALF), T - HALF)], ACC[1][:, 0:T - HALF], ACT.Copy, scale=gate)
                    fn(A[:, at(m * N + (HT + T), NS)], ACC[1][:, T - HALF:HALF], ACT.Copy
                       ).then_inc(s["acc_free"], 1)
                    acc.step()
                    ada(m + GT2)
            act.wait_ge(s["ada_free"], adas.value())
            done("out_ready")
            act.wait_ge(s["x1_ready"], 1)
            row_norms(x1, V(MG + D, D))
            pairs.n = WQ_PAIR - 1
            with loop(act, 4, (product, 8), (acc, 8), (pairs, 4)):
                for j in range(4):
                    act.wait_ge(s["pair_full"], pairs.value())
                    pairs.step()
                    read(0, qT[j % 2][:, 0:HALF], ACT.Copy)
                    act.wait_ge(s["product_done"], product.step())
                    fn(qT[j % 2][:, HALF:T], ACC[1][:, 0:T - HALF], ACT.Copy)
                    fn(qT[j % 2][:, T:640].rearrange("p (r n) -> p r n", r=4),
                       bc(ACC[1][:, T - HALF:HALF], 1, 4), ACT.Copy).then_inc(s["acc_free"], 1)
                    acc.step()
            act.wait_ge(s["dve_to_act"], from_dve.step())
            fn(V(HT + 4928, ROWT * SLOTS), V(HT + 4928, ROWT * SLOTS), ACT.Exp).then_inc(s["act_to_dve"], 1)
            vused = Count()

            for st in range(ROWT + 1):
                if st:
                    t, n = st - 1, (32 if st - 1 < 4 else 8)
                    w, rows, base = wts[t % 2], (128 if t < 4 else NS), (ident if t < 4 else fold)
                    act.wait_ge(s["w_ready"], t + 1)
                    with loop(act, n, (vused, 4)) as i:
                        for r in range(4):
                            act.wait_ge(s["v_used"], vused.step())
                            fn(diag[r][:, 0:rows], base, ACT.Copy, scale=w[:, at(i * 4 + r, 1)]
                               ).then_inc(s["diag_ready"], 1)
                if st < ROWT:
                    cols = 128 if st < 4 else 32
                    act.wait_ge(s["act_ready"], st + 1)
                    fn(wts[st % 2][:, 0:cols], acts[st % 2][:, 0:cols], ACT.Gelu).then_inc(s["gelu_ready"], 1)
                if st:
                    act.wait_ge(s["fin_in"], st)
                    fn(V(KT + 1153, 1), V(KT + 1152, 1), ACT.Sqrt).then_inc(s["fin_sum"], 1)

        @block.vector
        def _(dve):
            v = nc.vector
            tt, ts, cp = v.tensor_tensor, v.tensor_scalar, v.tensor_copy
            me = Own(dve, s["dve_step"])
            did, settle, then = me.did, me.settle, me.then
            pf = Own(dve, s["pair_free"], 2)
            full, acc = Count(), Count(2)
            dve.sem_inc(s["pair_free"], 2)
            dve.sem_inc(s["y_free"], 1)
            dve.sem_inc(s["piece_done"], 2)
            dve.sem_inc(s["u_used"], 4)
            from_act = Count()

            def take():
                X, Z = PAIR[full.n % 2]
                dve.wait_ge(s["pair_full"], full.step())
                return X, Z

            def signal(name):
                settle()
                pf.settle()
                dve.sem_inc(s[name], 1)

            def to_act():
                signal("dve_to_act")

            def act_back():
                dve.wait_ge(s["act_to_dve"], from_act.step())

            for k in range(2):
                did(v.memset(V(MG + 3328 + 1024 * k, 1024), 0.0))
                did(v.memset(V(MG + 6400 + 1024 * k, 1024), 0.0))
            signal("c_zeroed")
            dve.wait_ge(s["s5par_in"], 48)
            did(cp(A[0:32, par_rows + 256:par_rows + 384].rearrange("p (g q) -> p g q", g=2),
                   bc(A[0:32, par_rows + 384:par_rows + 386], 2, ST)))
            signal("rows_laid")
            X, _ = take()
            pf.did(cp(V(CS, KD * C9), X[:, 0:KD * C9]))
            signal("col_ready")
            X, Z = take()
            did(cp(V(BT, MODS), X[:, 0:MODS]))
            pf.did(cp(vecs, Z[:, 0:56]))
            signal("mods_ready")
            X, _ = take()
            are, aim, dt, lr, ph, phabs, q, t1, t2, t3, t4, fre, fim, den = (V(PH + 32 * j, 32) for j in range(14))
            for k, dst in enumerate((are, aim, dt)):
                last = cp(dst.rearrange("p (b a) -> p b a", b=NB),
                          X[:, 32 * k:32 * k + 32].rearrange("p (a b) -> p b a", b=NB))
                (did if k < 2 else pf.did)(last)
            X, Z = take()
            for k, (src, dst) in enumerate(((X, h0[0]), (Z, h0[1]))):
                for b in range(NB):
                    last = cp(dst[:, 64 * b:64 * b + 64].rearrange("p (a q) -> p q a", a=NA),
                              src[:, 0:256].rearrange("p (q a b) -> p b q a", q=SEQS, a=NA)[:, b])
                    (pf.did if k == 1 and b == 3 else did)(last)
            to_act()
            act_back()
            did(tt(lr, are, dt, ALU.mult))
            then(tt(t1, aim, dt, ALU.mult))
            then(ts(q, t1, 1.0 / (2.0 * math.pi), None, ALU.mult))
            then(ts(q, q, ROUND, None, ALU.add))
            then(ts(q, q, -ROUND, None, ALU.add))
            for part in TWO_PI:
                then(v.scalar_tensor_tensor(out=t1, in0=q, scalar=-part, in1=t1, op0=ALU.mult, op1=ALU.add))
            then(ts(ph, t1, 3.1415925, -3.1415925, ALU.min, ALU.max))
            then(ts(t2, ph, -1.0, None, ALU.mult))
            did(tt(phabs, ph, t2, ALU.max))
            to_act()
            act_back()
            did(tt(abr, lr, phabs, ALU.mult))
            did(tt(abi, lr, ph, ALU.mult))
            did(tt(t1, are, are, ALU.mult))
            did(tt(t2, aim, aim, ALU.mult))
            settle()
            then(tt(den, t1, t2, ALU.add))
            did(v.reciprocal(den, den))
            did(ts(q, abr, -1.0, None, ALU.add))
            settle()
            did(tt(t1, q, are, ALU.mult))
            did(tt(t2, abi, aim, ALU.mult))
            did(tt(t3, abi, are, ALU.mult))
            did(tt(t4, q, aim, ALU.mult))
            settle()
            did(tt(fre, t1, t2, ALU.add))
            did(tt(fim, t3, t4, ALU.subtract))
            settle()
            did(tt(fre, fre, den, ALU.mult))
            did(tt(fim, fim, den, ALU.mult))
            settle()
            dve.wait_ge(s["b_weights_in"], 32)
            byba = "p (a b) c -> p b a c"
            for k in range(2):
                m1, m2 = V(PH + 512, 512), V(PH + 1024, 512)
                for g in range(2):
                    r = slice(64 * g, 64 * g + 64)
                    for b in range(NB):
                        for f, src, dst in ((fre, b_nat[k], m1), (fim, b_nat[1 - k], m2)):
                            did(tt(dst[r, 128 * b:128 * b + 128].rearrange("p (a c) -> p a c", a=NA),
                                   src[r].rearrange(byba, b=NB)[:, b], bc(f[r, 8 * b:8 * b + 8], 2, GC), ALU.mult))
                settle()
                for g in range(2):
                    r = slice(64 * g, 64 * g + 64)
                    for b in range(NB):
                        did(tt(b_wide[k][r].rearrange(byba, b=NB)[:, b, :, 16 * g:16 * g + 16],
                               m1[r, 128 * b:128 * b + 128].rearrange("p (a c) -> p a c", a=NA),
                               m2[r, 128 * b:128 * b + 128].rearrange("p (a c) -> p a c", a=NA),
                               ALU.subtract if k == 0 else ALU.add))
                settle()
            signal("bb_ready")

            def row_norms(src, dst):
                act_back()
                then(ts(ss, ss, 1.0 / D, EPS, ALU.mult, ALU.add))
                did(v.reciprocal(rstd, ss))
                to_act()
                act_back()
                for t in range(ROWT):
                    did(ts(dst[:, t, :], src[:, t, :], rstd[:, t:t + 1], None, ALU.mult))
                signal("xn_ready")

            row_norms(x1, x1)
            for k in range(2):
                X, Z = take()
                did(ts(V(CT + 1024 * k, 512), X, (1.0, -1.0)[k], None, ALU.mult))
                pf.did(ts(V(CT + 1024 * k + 512, 512), Z, (1.0, -1.0)[k], None, ALU.mult))
            for k in range(2):
                X, Z = take()
                did(cp(V(BB + 1024 * k, 512), X))
                pf.did(cp(V(BB + 1024 * k + 512, 512), Z))

            def modulate(base, dst, gain, sc, sh):
                g = mod[:, sc:sc + KD, :]
                then(v.scalar_tensor_tensor(out=g, in0=g, scalar=1.0, in1=bc(gain, 2, C9),
                                            op0=ALU.add, op1=ALU.mult))
                with loop(dve, 8, (full, 2), (pf.count, 2), (me.count, 2)) as i:
                    for j in range(2):
                        k = i * 2 + j
                        X, Z = take()
                        did(ts(A[:, at(k * N + base, T)], X, A[:, at(k * C9 + (MOD + sc * C9), 1)],
                               A[:, at(k * C9 + (MOD + sh * C9), 1)], ALU.mult, ALU.add))
                        pf.did(cp(A[:, at(k * N + (base + T), NS)], Z[:, 0:NS]))
                settle()
                pf.settle()
                seq = dst[:, :, T:N].rearrange("p k (q t) -> p k q t", q=SEQS)
                then(tt(seq, seq, bc(mod[:, sc:sc + KD, 1:C9], 3, STEPS), ALU.mult))
                then(tt(seq, seq, bc(mod[:, sh:sh + KD, 1:C9], 3, STEPS), ALU.add))

            dve.wait_ge(s["mods_ready"], 2)
            modulate(HT, hT, g1T, SC1, SH1)
            signal("col_ready")

            assert full.n == S5_PAIR
            pw = [V(PH + 448 + 32 * j, 32) for j in range(6)]
            cs_, sn_ = V(PH + 64 + 96, 32), V(PH + 64 + 64, 32)
            tc, tsn = V3(E, 32, L), V3(E + 2048, 32, L)
            did(v.memset(tc[:, :, 0:1], 1.0))
            did(v.memset(tsn[:, :, 0:1], 0.0))
            did(cp(pw[0], cs_))
            did(cp(pw[1], sn_))
            settle()
            n = 1
            while n < L:
                sz = 32 * n
                w1, w2 = V3(PH + 1024, 32, n), V3(PH + 2048, 32, n)
                pr, pi = bc(pw[0], 2, n), bc(pw[1], 2, n)
                did(tt(w1, tc[:, :, 0:n], pr, ALU.mult))
                then(tt(w2, tsn[:, :, 0:n], pi, ALU.mult))
                did(tt(tc[:, :, n:2 * n], w1, w2, ALU.subtract))
                settle()
                did(tt(w1, tc[:, :, 0:n], pi, ALU.mult))
                then(tt(w2, tsn[:, :, 0:n], pr, ALU.mult))
                did(tt(tsn[:, :, n:2 * n], w1, w2, ALU.add))
                did(tt(pw[2], pw[0], pw[0], ALU.mult))
                did(tt(pw[3], pw[1], pw[1], ALU.mult))
                did(tt(pw[4], pw[0], pw[1], ALU.mult))
                settle()
                did(tt(pw[0], pw[2], pw[3], ALU.subtract))
                did(ts(pw[1], pw[4], 2.0, None, ALU.mult))
                settle()
                n *= 2
            did(cp(V3(E + 4096, 32, L), bc(lr, 2, L)))
            did(cp(V3(E + 6144, 32, NS), bc(lr, 2, NS)))
            did(v.memset(V(HL, 64), 0.0))
            settle()
            did(v.memset(V3(E + 4096, 32, L)[:, :, 0:1], 0.0))
            did(v.memset(V3(E + 6144, 32 * SEQS, STEPS)[:, :, 0:1], 0.0))
            settle()

            ydone = Count()

            def carry(hr, hi, cr, ci, w, br, bi):
                did(tt(w[0], br, hr, ALU.mult))
                did(tt(w[1], bi, hi, ALU.mult))
                did(tt(w[2], br, hi, ALU.mult))
                did(tt(w[3], bi, hr, ALU.mult))
                settle()
                did(tt(cr, w[0], w[1], ALU.subtract))
                did(tt(ci, w[2], w[3], ALU.add))
                settle()

            def unit(b, sz, view, cos, sin, cf, cr, ci, first, save):
                X, Z = take()
                br, bi = X[:, 0:sz], Z[:, 0:sz]
                w1, w2, w3, w4 = (w[:, 0:sz] for w in (W1, W2, W3, W4))
                hr, hi = (w[:, 0:sz] for w in HB[b % 2])
                did(tt(view(w1), view(br), cos, ALU.mult))
                did(tt(view(w2), view(bi), sin, ALU.mult))
                did(tt(view(w3), view(bi), cos, ALU.mult))
                pf.did(tt(view(w4), view(br), sin, ALU.mult))
                settle()
                pf.settle()
                did(tt(w1, w1, w2, ALU.add))
                did(tt(w3, w3, w4, ALU.subtract))
                settle()
                did(tt(first(w1), first(w1), cr, ALU.add))
                did(tt(first(w3), first(w3), ci, ALU.add))
                settle()
                did(v.tensor_tensor_scan(w2, cf, w1, 0.0, ALU.mult, ALU.add))
                did(v.tensor_tensor_scan(w4, cf, w3, 0.0, ALU.mult, ALU.add))
                settle()
                dve.wait_ge(s["y_done"], ydone.step())
                did(tt(view(w1), view(w2), cos, ALU.mult))
                did(tt(view(w3), view(w4), sin, ALU.mult))
                did(tt(view(hi), view(w4), cos, ALU.mult))
                settle()
                did(tt(hr, w1, w3, ALU.subtract))
                did(tt(view(w4), view(w2), sin, ALU.mult))
                settle()
                did(tt(hi, hi, w4, ALU.add))
                settle()
                did(cp(save[0], save[2](hr)))
                did(cp(save[1], save[2](hi)))
                dve.sem_inc(s["h_ready"], 1)
                settle()

            def outputs(chunk_columns, n):
                did(tt(W1[:, 0:NA * n].rearrange("p (a n) -> p a n", a=NA), chunk_columns, bc(dT, 2, n), ALU.mult))
                settle()
                dve.wait_ge(s["y_done"], ylast.step(4))
                tt(chunk_columns, W1[:, 0:NA * n].rearrange("p (a n) -> p a n", a=NA),
                   YB[:, 0:NA * n].rearrange("p (a n) -> p a n", a=NA), ALU.add).then_inc(s["y_free"], 1)
                dve.wait_ge(s["y_free"], yout.step())

            ylast, yout = Count(2), Count(1)

            def chunk(before):
                carry(hlr, hli, crr, cri, [V(PH + 32 * j, 32) for j in range(4)], abr, abi)
                for b in range(NB):
                    col = slice(8 * b, 8 * b + 8)
                    unit(b, 512, lambda w: w, tabc[:, b].rearrange("p a t -> p (a t)"),
                         tabs[:, b].rearrange("p a t -> p (a t)"), coef[:, b].rearrange("p a t -> p (a t)"),
                         crr[:, col], cri[:, col],
                         lambda w: w.rearrange("p (a t) -> p a t", a=NA)[:, :, 0],
                         (hlr[:, col], hli[:, col],
                          lambda w: w.rearrange("p (a t) -> p a t", a=NA)[:, :, L - 1]))
                    if b == 0 and before is not None:
                        outputs(before, L)

            dve.wait_ge(s["ua_ready"], 1)
            chunk(None)
            with loop(dve, CHUNKS - 1, (me.count, 75), (pf.count, 4), (full, 4), (ydone, 4), (ylast, 4),
                      (yout, 1)) as c:
                chunk(uaT[:, :, at(c * L, L)])
            abrS, abiS = bc(abr, 2, SEQS), bc(abi, 2, SEQS)

            def by_state(w):
                return w.rearrange("p (i q) -> p i q", q=SEQS)

            cS = (V(PH + 1280, 256), V(PH + 1792, 256))
            carry(by_state(h0[0]), by_state(h0[1]), by_state(cS[0]), by_state(cS[1]),
                  [by_state(V(PH + 256 * j, 256)) for j in range(4)], abrS, abiS)
            for b in range(NB):
                col = slice(64 * b, 64 * b + 64)
                unit(b, 256, lambda w: w.rearrange("p (a q t) -> p a q t", a=NA, q=SEQS),
                     bc(tabc[:, b, :, 0:STEPS], 2, SEQS), bc(tabs[:, b, :, 0:STEPS], 2, SEQS),
                     coefS[:, 256 * b:256 * b + 256], cS[0][:, col], cS[1][:, col],
                     lambda w: w.rearrange("p (i t) -> p i t", t=STEPS)[:, :, 0],
                     (h0[0][:, col], h0[1][:, col],
                      lambda w: w.rearrange("p (i t) -> p i t", t=STEPS)[:, :, STEPS - 1]))
                if b == 0:
                    outputs(uaT[:, :, T - L:T], L)
            outputs(uaT[:, :, T:N], NS)
            dve.wait_ge(s["y_free"], yout.value())
            dve.sem_inc(s["y_ready"], 1)
            signal("s5_done")
            for k, src in enumerate((hlr, hli)):
                did(cp(V(PH + 3072 + 32 * k, 32).rearrange("p (a b) -> p b a", b=NB),
                       src.rearrange("p (b a) -> p b a", b=NB)))
            for k in range(2):
                for b in range(NB):
                    did(cp(V(PH + 3136 + 256 * k, 256).rearrange("p (q a b) -> p b a q", q=SEQS, a=NA)[:, b],
                           h0[k][:, 64 * b:64 * b + 64].rearrange("p (a q) -> p a q", a=NA)))
            signal("rows_laid")
            X, Z = take()
            did(cp(A[0:32, PH:PH + 256], X[0:32, 0:256]))
            pf.did(cp(V(PH + 256, 512), Z))
            for rows, dst in ((BUF, out_prompt_rows), (NS, out_sample_rows)):
                X, Z = take()
                did(cp(dst[0:rows, 0:512], X[0:rows, :]))
                pf.did(cp(dst[0:rows, 512:1024], Z[0:rows, :]))
            signal("state_rows")
            dve.wait_ge(s["state_out"], 256)
            PA, PB = V3(PH, 2, T + BUF), V3(PH + 1054, 2, T + BUF)
            for g, win in enumerate(WINDOWS):
                u = ubT[:, 2 * g:2 * g + 2, 0:T]
                did(v.memset(PA[:, :, 0:BUF], 0.0))
                did(cp(PA[:, :, BUF:], u))
                settle()
                src, dst = PA, PB
                for lev in range(g + 1):
                    lo, sh = 2 ** (lev + 1) - 1, 2 ** lev
                    then(tt(dst[:, :, lo:], src[:, :, lo:], src[:, :, lo - sh:T + BUF - sh], ALU.add))
                    src, dst = dst, src
                then(tt(src[:, :, BUF:BUF + 16], src[:, :, BUF:BUF + 16], bc(corr[:, g, :], 1, 2), ALU.mult))
                then(v.scalar_tensor_tensor(out=u, in0=src[:, :, BUF:], scalar=1.0 / win, in1=u,
                                            op0=ALU.mult, op1=ALU.subtract))
            dve.wait_ge(s["glu_ready"], 1)
            then(tt(V(BB, KW * N), V(BB, KW * N), V(UA, KW * N), ALU.mult))
            signal("ya_ready")
            EX = V(PH + 2108, 1216).rearrange("p (a q e) -> p a q e", a=KW, q=SEQS)
            EB = [V(PH + 3324 + 304 * j, 304).rearrange("p (a q e) -> p a q e", a=2, q=SEQS) for j in range(2)]
            X, Z = take()
            for k, src in enumerate((X, Z)):
                last = cp(EX[:, 4 * k:4 * k + 4, :, 0:BUF],
                          src[:, 0:480].rearrange("p (a q e) -> p a q e", a=4, q=SEQS))
                (did if k == 0 else pf.did)(last)
            for a in range(KW):
                did(cp(EX[:, a, :, BUF:], ubT[:, a, T:N].rearrange("p (q t) -> p q t", q=SEQS)))
            settle()
            pf.settle()
            for g, win in enumerate(WINDOWS):
                src, dst = EX[:, 2 * g:2 * g + 2], EB[0]
                for lev in range(g + 1):
                    lo, sh = 2 ** (lev + 1) - 1, 2 ** lev
                    then(tt(dst[:, :, :, lo:], src[:, :, :, lo:], src[:, :, :, lo - sh:19 - sh], ALU.add))
                    src, dst = dst, EB[(lev + 1) % 2]
                then(ts(src[:, :, :, BUF:], src[:, :, :, BUF:], 1.0 / win, None, ALU.mult))
                for a in range(2):
                    u = ubT[:, 2 * g + a, T:N].rearrange("p (q t) -> p q t", q=SEQS)
                    did(tt(u, src[:, a, :, BUF:], u, ALU.subtract))
                settle()
            signal("pooled")

            acc.n = 2 + 2 * (8 + 8 + 16 + 8 + 8)
            def gated(m, h, gate=None):
                dst = A[:, at(m * N + (MG + HALF * h), HALF)]
                if gate is None:
                    dve.wait_ge(s["acc_free"], acc.step())
                    tt(dst, dst, piece[h], ALU.mult).then_inc(s["piece_done"], 1)
                else:
                    then(tt(piece[h], piece[h], gate, ALU.mult))
                    tt(dst, dst, piece[h], ALU.add).then_inc(s["piece_done"], 1)

            with loop(dve, 4, (acc, 8)) as i:
                for m in range(4):
                    for h in range(2):
                        gated(i * 4 + m, h)
            with loop(dve, 8, (acc, 8), (me.count, 4)) as i:
                acc.step(4)
                for m in range(2):
                    for h in range(2):
                        dve.wait_ge(s["acc_free"], acc.step())
                        gated(i * 2 + m, h, sig[2 * m + h])
            dve.wait_ge(s["piece_done"], 2 + 64)
            signal("merged_ready")

            dve.wait_ge(s["out_ready"], 1)
            seq = hT[:, :, T:N].rearrange("p k (q t) -> p k q t", q=SEQS)
            then(tt(seq, seq, bc(mod[:, GT1:GT1 + KD, 1:C9], 3, STEPS), ALU.mult))
            did(cp(V(MG, D).rearrange("p (k r n) -> p k r n", k=KD, r=4), bc(hT[:, :, T:N], 2, 4)))
            signal("expand_ready")
            dve.wait_ge(s["x_in"], 160)

            def rows_from_pairs(dst, op):
                with loop(dve, 8, (full, 2), (pf.count, 2), (me.count, 2)) as i:
                    for j in range(2):
                        X, Z = take()
                        x4 = dst[:, 0:4, at((i * 2 + j) * 128, 128)]
                        xs = dst[:, 4, at((i * 2 + j) * 128, 128)]
                        X4 = X.rearrange("p (t n) -> p t n", t=4)
                        if op:
                            did(tt(x4, x4, X4, ALU.add))
                            pf.did(tt(xs, xs, Z[:, 0:128], ALU.add))
                        else:
                            did(cp(x4, X4))
                            pf.did(cp(xs, Z[:, 0:128]))

            rows_from_pairs(x1, True)
            signal("x1_ready")
            row_norms(x1, xn)
            modulate(MG, mT, g2T, SC2, SH2)
            did(cp(V(HT, D).rearrange("p (k r n) -> p k r n", k=KD, r=4), bc(mT[:, :, T:N], 2, 4)))
            signal("expand_ready")
            rows_from_pairs(xn, False)
            for half in range(2):
                X, Z = take()
                did(cp(V(KT + 1024 * half, 512), X))
                pf.did(cp(V(KT + 1024 * half + 512, 512), Z))
            signal("keys_laid")

            tsc = V(TS, ROWT * 32).rearrange("p (t h k) -> p t h k", t=ROWT, h=2)
            tix = V(TI, ROWT * 32).bitcast(U32).rearrange("p (t h k) -> p t h k", t=ROWT, h=2)
            S2 = V3(HT + 1280, ROWT, 128)
            comb = V4(HT + 1920, ROWT, 16, 16)
            tif = V(HT + 3200, ROWT * 32).rearrange("p (t h k) -> p t h k", t=ROWT, h=2)
            bj = V(HT + 3360, 80).bitcast(U32)
            bj3 = bj.rearrange("p (t k) -> p t k", t=ROWT)
            half_i = [V(HT + 3440 + 80 * j, 80).bitcast(U32) for j in range(2)]
            half_f = [V(HT + 3600 + 80 * j, 80) for j in range(2)]
            place = [V(HT + 3760 + 80 * j, 80) for j in range(2)]
            rest = V3(HT + 5280, ROWT, 256)
            hot = V(HT + 3920, 1280).rearrange("p (n a) -> p n a", a=16)
            ids = ix.rearrange("p (t n) -> p t n", t=ROWT)
            best = gates.rearrange("p (t n) -> p t n", t=ROWT)
            assert full.n == WQ_PAIR

            def top16(src, spare, score, index):
                def stand():
                    settle()
                    dve.sem_inc(s["dve_stood"], 1)

                stand()
                for t in range(ROWT):
                    did(v.max(score[t][:, 0:8], src[t]))
                stand()
                for t in range(ROWT):
                    did(v.max_index(index[t][:, 0:8], score[t][:, 0:8], src[t]))
                    did(v.match_replace(spare[t], score[t][:, 0:8], src[t], LOW))
                stand()
                for t in range(ROWT):
                    did(v.max(score[t][:, 8:16], spare[t]))
                stand()
                for t in range(ROWT):
                    did(v.max_index(index[t][:, 8:16], score[t][:, 8:16], spare[t]))
                stand()

            with loop(dve, 8, (full, 2), (pf.count, 2), (me.count, 93)) as hd:
                for half in range(2):
                    X, Z = take()
                    src = [X[:, 128 * t:128 * t + 128] for t in range(4)] + [Z[:, 0:128]]
                    top16(src, [S2[:, t, :] for t in range(ROWT)], [tsc[:, t, half, :] for t in range(ROWT)],
                          [tix[:, t, half, :] for t in range(ROWT)])
                    dve.sem_inc(s["pair_free"], 1)
                    pf.count.step()
                for t in range(ROWT):
                    did(tt(comb[:, t], bc(tsc[:, t, 0, :], 2, 16), bc(tsc[:, t, 1, :], 1, 16), ALU.add))
                did(cp(tif, tix))
                settle()
                sc = V(HT + 5200, 80).rearrange("p (t k) -> p t k", t=ROWT)
                flat = [comb[:, t].rearrange("p a b -> p (a b)") for t in range(ROWT)]
                top16(flat, [rest[:, t, :] for t in range(ROWT)], [sc[:, t, :] for t in range(ROWT)],
                      [bj3[:, t, :] for t in range(ROWT)])
                did(cp(best[:, :, at(hd * 16, 16)], sc))
                did(ts(half_i[0], bj, 4, None, ALU.logical_shift_right))
                did(ts(half_i[1], bj, 15, None, ALU.bitwise_and))
                settle()
                for k in range(2):
                    did(cp(half_f[k], half_i[k]))
                settle()
                for k in range(2):
                    then(tt(hot, bc(half_f[k], 2, 16), bc(iota16, 1, 80), ALU.is_equal))
                    then(tt(hot.rearrange("p (t k) a -> p t k a", t=ROWT),
                            hot.rearrange("p (t k) a -> p t k a", t=ROWT), bc(tif[:, :, k, :], 2, 16), ALU.mult))
                    then(v.tensor_reduce(place[k], hot, AX.X, ALU.add))
                did(v.scalar_tensor_tensor(out=ids[:, :, at(hd * 16, 16)],
                                           in0=place[0].rearrange("p (t k) -> p t k", t=ROWT), scalar=128.0,
                                           in1=place[1].rearrange("p (t k) -> p t k", t=ROWT),
                                           op0=ALU.mult, op1=ALU.add))
                settle()
            ex = V3(HT + 4928, ROWT * HEADS, 16)
            b3 = gates.rearrange("p (n k) -> p n k", k=16)
            did(tt(ex, b3, bc(b3[:, :, 0], 2, 16), ALU.subtract))
            to_act()
            did(cp(V(HT, D).rearrange("p (k n) -> p k n", k=KD), bc(mod[:, GT2:GT2 + KD, 0], 2, 128)))
            for q in range(SEQS):
                did(cp(V3(HT + D, KD, NS)[:, :, STEPS * q:STEPS * q + STEPS],
                       bc(mod[:, GT2:GT2 + KD, 1 + q], 2, STEPS)))
            signal("expand_ready")
            act_back()
            sums = V(HT + 5760, 40)
            then(v.tensor_reduce(sums, ex, AX.X, ALU.add))
            then(v.reciprocal(sums, sums))
            did(tt(b3, ex, bc(sums, 2, 16), ALU.mult))
            settle()
            for r in range(4):
                p4 = slice(32 * r, 32 * r + 32)
                did(cp(ixS[p4], ix[p4, 4 * SLOTS + 32 * r:4 * SLOTS + 32 * r + 32]))
                did(cp(gS[p4], gates[p4, 4 * SLOTS + 32 * r:4 * SLOTS + 32 * r + 32]))
            signal("idx_ready")
            for dst, rows in ((gt2P, 128), (gt2S, NS)):
                for q in range(2):
                    X, Z = take()
                    did(cp(dst[0:rows, 1024 * q:1024 * q + 512], X[0:rows, :]))
                    pf.did(cp(dst[0:rows, 1024 * q + 512:1024 * q + 1024], Z[0:rows, :]))
            pf.settle()
            dve.sem_inc(s["peer_free"], 2)

            ulap = Count()
            ms, root = V(KT + 1152, 1), V(KT + 1153, 1)
            done_v = 4
            for st in range(ROWT + 1):
                if st < ROWT:
                    a_, n = acts[st % 2], (32 if st < 4 else 8)
                    with loop(dve, n, (ulap, 1)) as i:
                        for r in range(4):
                            dve.wait_ge(u_full[r], ulap.value() * 16 + 16)
                            v.scalar_tensor_tensor(out=ubuf[r], in0=ubuf[r], scalar=1.0, in1=xn[:, st, :],
                                                   op0=ALU.mult, op1=ALU.mult, accum_out=a_[:, at(i * 4 + r, 1)]
                                                   ).then_inc(s["u_used"], 1)
                        ulap.step()
                    dve.wait_ge(s["u_used"], 4 + (128 * (st + 1) if st < 4 else 512 + 32))
                    dve.sem_inc(s["act_ready"], 1)
                    dve.wait_ge(s["gelu_ready"], st + 1)
                    w = wts[st % 2][:, 0:4 * n]
                    did(tt(w, w, gates[:, SLOTS * st:SLOTS * st + SLOTS] if st < 4 else gS, ALU.mult))
                    signal("w_ready")
                if st:
                    t = st - 1
                    rows, gt2 = (128, gt2P) if t < 4 else (NS, gt2S)
                    done_v += 128 if t < 4 else 32
                    dve.wait_ge(s["v_used"], done_v)
                    if t == 0:
                        dve.wait_ge(s["gfinal_in"], 16)
                    f, x = fin[0:rows], x1[0:rows, t, :]
                    then(tt(f, psum4[t % 2][0:rows, :], gt2[0:rows], ALU.mult))
                    dve.sem_inc(s["peer_free"], 1)
                    then(tt(x, x, f, ALU.add))
                    then(v.scalar_tensor_tensor(out=f, in0=x, scalar=1.0, in1=x, op0=ALU.mult, op1=ALU.mult,
                                                accum_out=ms[0:rows]))
                    then(ts(ms[0:rows], ms[0:rows], 1.0 / D, EPS, ALU.mult, ALU.add))
                    then(v.reciprocal(ms[0:rows], ms[0:rows]))
                    dve.sem_inc(s["fin_in"], 1)
                    dve.wait_ge(s["fin_sum"], t + 1)
                    then(v.scalar_tensor_tensor(out=x, in0=x, scalar=root[0:rows], in1=gfin[0:rows],
                                                op0=ALU.mult, op1=ALU.mult))
                    dve.sem_inc(s["fin_row"], 1)


INPUTS = {
    "x_prompt": None, "x_sample": None, "state_s5_re": (SEQS, G, ST), "state_s5_im": (SEQS, G, ST),
    "state_pool": (SEQS, BUF, W), "c_prompt": None, "c_sample": None, "w_ada": (D, 6 * D), "b_ada": (6 * D,),
    "g_norm1": (D,), "g_norm2": (D,), "w_in": (D, 3 * D), "s5_a_re": (G, ST), "s5_a_im": (G, ST),
    "s5_log_dt": (G,), "s5_b_re": (G, ST, GC), "s5_b_im": (G, ST, GC), "s5_c_re": (G, GC, ST),
    "s5_c_im": (G, GC, ST), "s5_d": (W,), "w_glu": (W, W), "b_glu": (W,), "w_pool": (4, 256, 256),
    "pool_scale": (W,), "w_proj_a": (W, D), "w_proj_b": (W, D), "w_out": (D, D), "peer_wq": (D, D),
    "peer_keys": (HEADS, 2, 128, 128), "peer_u": (16384, D), "peer_v": (16384, D), "g_final": None,
}
OUTPUTS = {
    "y_prompt": (1, T, D), "y_sample": (SEQS, STEPS, D), "new_s5_re_prompt": (G, ST), "new_s5_im_prompt": (G, ST),
    "new_pool_prompt": (BUF, W), "new_s5_re_sample": (SEQS, G, ST), "new_s5_im_sample": (SEQS, G, ST),
    "new_pool_sample": (SEQS, BUF, W),
}
RETURNED = [(1, T, D), (SEQS, STEPS, D), (1, 1, G, ST), (1, 1, G, ST), (1, 1, BUF, W), (1, SEQS, G, ST),
            (1, SEQS, G, ST), (1, SEQS, BUF, W)]


def constants():
    c = np.zeros((P, NCON), np.float32)
    c[:, 0:128] = np.eye(P)
    c[:, 128:144] = np.arange(16)
    for g, w in enumerate(WINDOWS):
        c[:, 144 + 16 * g:160 + 16 * g] = w / np.minimum(np.arange(16) + 1, w)
    c[:, 208:240] = np.tile(np.eye(NS), (4, 1))
    c[:, 240] = math.pi / 2
    return c


def kernel(**inputs):
    import concourse.bacc as bacc
    from concourse.bass_utils import run_bass_kernel_spmd

    nc = bacc.Bacc("TRN2", target_bir_lowering=False, num_devices=1)
    arrays, ins, outs = {}, {}, {}
    for name, shape in INPUTS.items():
        a = np.ascontiguousarray(inputs[name])
        arrays[name] = a if shape is None else a.reshape(shape)
    arrays["consts"] = constants()
    for name, a in arrays.items():
        ins[name] = nc.dram_tensor(name, a.shape, F32, kind="ExternalInput").ap()
    for name, shape in OUTPUTS.items():
        outs[name] = nc.dram_tensor(name, shape, F32, kind="ExternalOutput").ap()
    layer(nc, ins, outs)
    r = run_bass_kernel_spmd(nc, [arrays], core_ids=[0]).results[0]
    return tuple(r[name].reshape(shape) for name, shape in zip(OUTPUTS, RETURNED))
```

```python
import math
from contextlib import ExitStack, contextmanager

import numpy as np
import concourse.bass as bass
from concourse import mybir

F32 = mybir.dt.float32
U32 = mybir.dt.uint32
ALU = mybir.AluOpType
ACT = mybir.ActivationFunctionType
AX = mybir.AxisListType

P = 128
D = 2048
KD = D // P
T = 512
SEQS, STEPS = 8, 4
NS = SEQS * STEPS
N = T + NS
HALF = N // 2
ROWT = T // P + 1
W = D // 2
KW = W // P
G, GC, ST = 64, 16, 64
L = 64
CHUNKS = T // L
NB, NA = 4, 8
BUF = 15
WINDOWS = (2, 4, 8, 16)
MODS = 6 * KD
SH1, SC1, GT1, SH2, SC2, GT2 = (KD * i for i in range(6))
C9 = 1 + SEQS
HEADS, TOPK = 8, 16
SLOTS = HEADS * TOPK
SUMS = 4 * 16 + 12 * 4
EPS = 1e-6
LOW = -3.0e38
TWO_PI = (6.28125, 1.9350051879882812e-3, 3.019916e-7)
ROUND = 12582912.0

SLAB = 2048
RING = 0
HT = RING + 4 * SLAB
MG = HT + KD * N
UA = MG + KD * N
UB = UA + KW * N
E = UB + KW * N
BB = E + 7168
CT = BB + 2048
US = CT + 2048
PH = US + 512
MOD = PH + 4096 + C9
CON = MOD + MODS * C9
NCON = 128 + 16 + 64 + 32 + 1
BT = CON + NCON
VT = BT + MODS
CS = VT + 56
AB = CS + KD * C9
CR = AB + 64
HL = CR + 64
H0 = HL + 64
SS = H0 + 512
AT = SS + 8 + ROWT
UX = AT + 256
ID2 = UX + 8
AR = ID2 + 2 * 256
ARENA = AR + 128

X1 = UA
XN = X1 + ROWT * D
KT = PH
PICK = KT + 1160
BEST = PH + 2048
ID = [BEST + (ROWT + t) * 256 for t in range(3)] + [ID2, ID2 + 256]

S5_PAIR = 4 + 4 + KD
WQ_PAIR = S5_PAIR + 4 * (CHUNKS + 1) + 1 + 2 + 1 + 3 * KD + 2

SEMS = """consts_in c_in vec_in s5par_in h0_in c_zeroed c_weights_in b_weights_in x_in wpool_in pool_in keys_in
gfinal_in silu_done pair_full pair_free product_done acc_free ada_free staged h_ready y_done y_free act_step
dve_step dve_to_act act_to_dve mods_ready col_ready ua_ready ub_ready bb_ready s5_done y_ready z_ready
glu_ready pooled yb_ready ya_ready piece_done merged_ready out_ready rows_laid state_rows state_out x1_ready
head_ready idx_ready idx_staged u_used v_used act_ready gelu_ready w_ready diag_ready peer_free fin_in fin_sum fin_row
fin_out keys_laid expand_ready xn_ready dve_stood pool_stood""".split()


class Count:

    def __init__(self, start=0):
        self.n, self.i, self.per = start, None, 0

    def step(self, k=1):
        self.n += k
        return self.value()

    def value(self):
        return self.n if self.i is None else self.n + self.i * self.per


class Own:

    def __init__(self, eng, sem, start=0):
        self.eng, self.sem, self.count = eng, sem, Count(start)

    def did(self, instruction):
        instruction.then_inc(self.sem, 1)
        self.count.step()

    def settle(self):
        self.eng.wait_ge(self.sem, self.count.value())

    def then(self, instruction):
        self.did(instruction)
        self.settle()


@contextmanager
def loop(eng, times, *counts):
    starts = [c.n for c, _ in counts]
    with eng.Fori(0, times) as i:
        for c, per in counts:
            c.i, c.per = i, per
        yield i
    for k, ((c, per), n) in enumerate(zip(counts, starts)):
        assert c.n - n == per, (k, c.n - n, per)
        c.n, c.i = n + per * times, None


def bc(ap, axis, count):
    ap = ap.unsqueeze(axis)
    shape = list(ap.shape)
    shape[axis] = count
    return ap.to_broadcast(shape)


def at(start, n):
    return bass.ds(start, n)


def layer(nc, i_, o_):
    with ExitStack() as ctx:
        A = ctx.enter_context(nc.sbuf_tensor("arena", [P, ARENA], F32))
        ps = ctx.enter_context(nc.psum_tensor("banks", [P, 4096], F32))
        s = {n: ctx.enter_context(nc.semaphore(n)) for n in SEMS}
        ring_full = [ctx.enter_context(nc.semaphore(f"ring_full{j}")) for j in range(4)]
        u_full = [ctx.enter_context(nc.semaphore(f"u_full{j}")) for j in range(4)]
        v_full = [ctx.enter_context(nc.semaphore(f"v_full{j}")) for j in range(4)]

        def V(off, n):
            return A[:, off:off + n]

        def V3(off, a, b):
            return V(off, a * b).rearrange("p (a b) -> p a b", a=a)

        def V4(off, a, b, c):
            return V(off, a * b * c).rearrange("p (a b c) -> p a b c", a=a, b=b)

        ident, iota16, corr = V(CON, 128), V(CON + 128, 16), V3(CON + 144, 4, 16)
        fold, half_pi = V(CON + 208, 32), V(CON + 240, 1)
        vecs = V(VT, 56)
        g1T, g2T = vecs[:, 0:16], vecs[:, 16:32]
        bgluT, pscaleT, dT = vecs[:, 32:40], vecs[:, 40:48], vecs[:, 48:56]
        mod = V3(MOD, MODS, C9)
        cT = V3(CS, KD, C9)
        ada_rows = V(AR, 128)
        ss, rstd = V(SS, ROWT), V(SS + 8, ROWT)
        bank = [ps[:, 512 * j:512 * j + 512] for j in range(8)]
        ACC, ADA, YB = (bank[0], bank[1]), bank[2], bank[7]
        PAIR = ((bank[3], bank[4]), (bank[5], bank[6]))
        slab16 = [V3(RING + SLAB * j, 16, 128) for j in range(4)]
        slab8 = [V3(RING + SLAB * j, 8, 256) for j in range(4)]
        hT, mT, uaT, ubT = V3(HT, KD, N), V3(MG, KD, N), V3(UA, KW, N), V3(UB, KW, N)
        ybT, yaT, wpool = V3(E, KW, N), V3(BB, KW, N), V3(E + KW * N, 8, 256)
        tabc, tabs, coef = V4(E, NB, NA, L), V4(E + 2048, NB, NA, L), V4(E + 4096, NB, NA, L)
        coefS = V(E + 6144, 1024)
        BBT = (V3(BB, NA, 128), V3(BB + 1024, NA, 128))
        CTT = (V3(CT, NA, 128), V3(CT + 1024, NA, 128))
        ustage = V3(US, NA, L)
        W1, W2, W3, W4 = (V(PH + 512 * j, 512) for j in range(4))
        HB = [(V(PH + 2048 + 1024 * j, 512), V(PH + 2560 + 1024 * j, 512)) for j in range(2)]
        abr, abi, crr, cri, hlr, hli = (V(AB + 32 * j, 32) for j in range(6))
        h0 = (V(H0, 256), V(H0 + 256, 256))
        c_rows, vec_rows, par_rows = MG, MG + D, MG + D + 256
        h0_rows = (V3(MG + 2816, 2, 128), V3(MG + 3072, 2, 128))
        c_wide = (V3(MG + 3328, NA, 128), V3(MG + 4352, NA, 128))
        b_nat = (V3(MG + 5376, 32, GC), V3(MG + 5888, 32, GC))
        b_wide = (V3(MG + 6400, 32, 32), V3(MG + 7424, 32, 32))
        x1, xn = V3(X1, ROWT, D), V3(XN, ROWT, D)
        out_prompt_rows, out_sample_rows = V(PH + 1024, 1024), V(PH + 2048, 1024)
        piece = (V(PH, HALF), V(PH + HALF, HALF))
        sig = [V(PH + (2 + j) * HALF, HALF) for j in range(4)]
        keys_nat = V3(HT + 3648, 16, 128)
        ids = [V(ID[t], SLOTS).bitcast(U32) for t in range(ROWT)]
        best = [V(BEST + 256 * t, SLOTS) for t in range(ROWT)]
        qT = (V(HT, 544 + 96), V(HT + 640, 640))
        ubuf = [V(RING + D * j, D) for j in range(4)]
        ubuf1 = [V(HT + 4608, D), V(HT + 6656, D)] + ubuf[2:]
        vbuf = [V(HT + D * j, D) for j in range(4)]
        gfin, gt2P, gt2S, fin = (V(MG + D * j, D) for j in range(4))
        acts = [V(AT + 128 * j, 128) for j in range(2)]
        wts = [V(KT + 256 + 128 * j, 128) for j in range(2)]
        diag = [V(KT + 512 + 128 * j, 128) for j in range(4)]
        ixS, gS = V(KT + 1024, 32).bitcast(U32), V(KT + 1056, 32)
        expo, sums = V(PICK + 736, 128), V(PICK + 864, 8)
        uix, vix = V(UX, 4).bitcast(U32), V(UX + 4, 4).bitcast(U32)
        psum4 = [ps[:, 0:2048], ps[:, 2048:4096]]

        block = ctx.enter_context(nc.Block())

        @block.sync
        def _(sp):
            def blocks(name):
                return i_[name].rearrange("(k p) n -> p k n", p=P)

            w_in, w_ada, w_out, w_q = (blocks(n) for n in ("w_in", "w_ada", "w_out", "peer_wq"))
            w_glu, w_pa, w_pb = (blocks(n) for n in ("w_glu", "w_proj_a", "w_proj_b"))
            history = [None] * 4

            def load_rows():
                sp.dma_start(x1[:, 0:4, :], i_["x_prompt"].rearrange("b (t p) d -> (b p) t d", p=P)
                             ).then_inc(s["x_in"], 16)
                for r in range(4):
                    sp.dma_start(A[32 * r:32 * r + 32, X1 + 4 * D:X1 + 5 * D],
                                 i_["x_sample"].rearrange("s t d -> (s t) d")).then_inc(s["x_in"], 16)

            def laps(times, slots, base):
                total = sum(x[4] for x in slots)
                read = [sum(x[4] for x in slots[:j + 1]) for j in range(len(slots))]

                def one(i, finished):
                    for j, (w, cols, m0, step, _) in enumerate(slots):
                        if finished[j] is not None:
                            sp.wait_ge(s["product_done"], finished[j])
                        sp.dma_start((slab16 if cols == 128 else slab8)[j],
                                     w[:, :, at((i * step + m0) * cols, cols)]).then_inc(ring_full[j], 16)

                one(0, history)
                if times > 1:
                    with sp.Fori(1, times) as i:
                        one(i, [i * total + (base - total + r) for r in read])
                for j, r in enumerate(read):
                    history[j] = base + (times - 1) * total + r
                return base + times * total

            def pairs(w, m0, mods, cols=128, products=2):
                return [(w, cols, m0, 2, products), (w_ada, 128, mods, 2, 1),
                        (w, cols, m0 + 1, 2, products), (w_ada, 128, mods + 1, 2, 1)]

            sp.dma_start(V(CON, NCON), i_["consts"]).then_inc(s["consts_in"], 16)
            sp.dma_start(A[0:1, c_rows:c_rows + D], i_["c_prompt"]).then_inc(s["c_in"], 16)
            sp.dma_start(A[1:C9, c_rows:c_rows + D], i_["c_sample"]).then_inc(s["c_in"], 16)
            sp.dma_start(A[0:MODS, vec_rows:vec_rows + 128], i_["b_ada"].rearrange("(m q) -> m q", q=P)
                         ).then_inc(s["vec_in"], 16)
            r = 0
            for name, rows in (("g_norm1", KD), ("g_norm2", KD), ("b_glu", KW), ("pool_scale", KW), ("s5_d", KW)):
                sp.dma_start(A[r:r + rows, vec_rows + 128:vec_rows + 256], i_[name].rearrange("(m q) -> m q", q=P)
                             ).then_inc(s["vec_in"], 16)
                r += rows
            b = laps(1, [(w_ada, 128, j, 4, 1) for j in range(4)], 0)
            load_rows()
            b = laps(7, [(w_ada, 128, 4 + j, 4, 1) for j in range(4)], b)
            b = laps(4, pairs(w_in, 0, GT1), b + 1)
            b = laps(4, pairs(w_in, 8, GT1 + 8), b)
            b = laps(8, pairs(w_in, 32, SH2), b)
            b = laps(1, [(w_glu, 256, j, 4, 4) for j in range(4)], b)
            sp.wait_ge(s["s5_done"], 1)
            sp.dma_start(A[0:SEQS * BUF, E:E + W], i_["state_pool"].rearrange("s r c -> (s r) c")
                         ).then_inc(s["pool_in"], 16)
            sp.dma_start(wpool, i_["w_pool"].rearrange("g (k p) n -> p (g k) n", p=P)).then_inc(s["wpool_in"], 16)
            b += 2 * KW
            b = laps(4, pairs(w_pb, 0, SC2, 256, 4), b)
            b = laps(8, [(w_in, 128, 16, 2, 2), (w_ada, 128, SC2 + 8, 1, 1),
                         (w_in, 128, 17, 2, 2), (w_pa, 256, 0, 1, 4)], b)
            b = laps(1, pairs(w_out, 0, GT2), b)
            sp.wait_ge(s["merged_ready"], 1)
            load_rows()
            b = laps(7, pairs(w_out, 2, GT2 + 2), b)
            laps(8, [(w_q, 128, j, 2, 2) for j in range(2)], b + 1)
            for t in range(ROWT):
                sp.wait_ge(s["fin_row"], t + 1)
                if t < 4:
                    sp.dma_start(o_["y_prompt"].rearrange("b (t p) d -> (b p) t d", p=P)[:, t, :], x1[:, t, :]
                                 ).then_inc(s["fin_out"], 16)
                else:
                    sp.dma_start(o_["y_sample"].rearrange("s t d -> (s t) d"), A[0:NS, X1 + 4 * D:X1 + 5 * D]
                                 ).then_inc(s["fin_out"], 16)
            sp.wait_ge(s["fin_out"], 16 * ROWT)

        @block.gpsimd
        def _(pool):
            dma = pool.dma_start
            for k, name in enumerate(("s5_a_re", "s5_a_im")):
                dma(A[0:32, par_rows + 128 * k:par_rows + 128 * k + 128],
                    i_[name].rearrange("(i g) q -> i (g q)", g=2)).then_inc(s["s5par_in"], 16)
            dma(A[0:32, par_rows + 384:par_rows + 386], i_["s5_log_dt"].rearrange("(i g) -> i g", g=2)
                ).then_inc(s["s5par_in"], 16)
            for k, name in enumerate(("state_s5_re", "state_s5_im")):
                rows = i_[name].rearrange("(u s) (i g) q -> u (s i) (g q)", u=2, g=2)
                for u in range(2):
                    dma(h0_rows[k][:, u, :], rows[u]).then_inc(s["h0_in"], 16)
            for k, name in enumerate(("s5_b_re", "s5_b_im")):
                dma(b_nat[k], i_[name].rearrange("(i g) q c -> (g q) i c", g=2)).then_inc(s["b_weights_in"], 16)
            pool.wait_ge(s["c_zeroed"], 1)
            for k, name in enumerate(("s5_c_re", "s5_c_im")):
                src = i_[name].rearrange("(a b g) c q -> b g c a q", b=NB, g=2)
                for b in range(NB):
                    for g in range(2):
                        r = 32 * b + 16 * g
                        dma(c_wide[k][r:r + 16, :, 64 * g:64 * g + 64], src[b, g]).then_inc(s["c_weights_in"], 16)
            dma(o_["new_pool_sample"][:, 0:BUF - STEPS, :], i_["state_pool"][:, STEPS:BUF, :]
                ).then_inc(s["state_out"], 16)
            pool.wait_ge(s["state_rows"], 1)
            for k, name in enumerate(("new_s5_re_prompt", "new_s5_im_prompt")):
                dma(o_[name].rearrange("(i g) q -> i (g q)", g=2), A[0:32, PH + 128 * k:PH + 128 * k + 128]
                    ).then_inc(s["state_out"], 16)
            for k, name in enumerate(("new_s5_re_sample", "new_s5_im_sample")):
                rows = o_[name].rearrange("(u s) (i g) q -> u (s i) (g q)", u=2, g=2)
                for u in range(2):
                    dma(rows[u], V(PH + 256 + 256 * k + 128 * u, 128)).then_inc(s["state_out"], 16)
            dma(o_["new_pool_prompt"], out_prompt_rows[0:BUF, :]).then_inc(s["state_out"], 16)
            for q in range(SEQS):
                dma(o_["new_pool_sample"][q, BUF - STEPS:BUF, :],
                    out_sample_rows[STEPS * q:STEPS * q + STEPS, :]).then_inc(s["state_out"], 16)
            pool.wait_ge(s["state_out"], 16 * 16)
            pool.wait_ge(s["x1_ready"], 1)
            dma(keys_nat, i_["peer_keys"].rearrange("h k m d -> m (h k) d")).then_inc(s["keys_in"], 16)

            staged, used = Count(), {"u": Count(), "v": Count()}
            side = {"u": (i_["peer_u"], ubuf, uix, u_full, s["u_used"]),
                    "v": (i_["peer_v"], vbuf, vix, v_full, s["v_used"])}

            def gather(kind, r, column, early=False):
                table, buf, stage, full, freed = side[kind]
                if early:
                    buf = ubuf1
                pool.wait_ge(freed, used[kind].step())
                nc.gpsimd.tensor_copy(stage[:, r:r + 1], column).then_inc(s["idx_staged"], 1)
                pool.wait_ge(s["idx_staged"], staged.step())
                pool.sem_inc(s["pool_stood"], 1)
                nc.gpsimd.indirect_dma_start(
                    buf[r], None, table, bass.IndirectOffsetOnAxis(ap=stage[:, r:r + 1], axis=0),
                ).then_inc(full[r], 16)

            heads = Count()
            with loop(pool, HEADS - 1, (staged, TOPK), (used["u"], TOPK), (heads, 1)) as hd:
                pool.wait_ge(s["head_ready"], heads.step())
                for k in range(TOPK):
                    gather("u", k % 4, ids[0][:, at(hd * TOPK + k, 1)], early=True)
            pool.wait_ge(s["head_ready"], heads.step())
            for k in range(TOPK):
                gather("u", k % 4, ids[0][:, SLOTS - TOPK + k:SLOTS - TOPK + k + 1])
            dma(gfin, i_["g_final"].partition_broadcast(P)).then_inc(s["gfinal_in"], 16)
            for t in range(1, 4):
                with loop(pool, HEADS, (staged, 2 * TOPK), (used["u"], TOPK), (used["v"], TOPK), (heads, 1)) as hd:
                    pool.wait_ge(s["head_ready"], heads.step())
                    for k in range(TOPK):
                        gather("u", k % 4, ids[t][:, at(hd * TOPK + k, 1)])
                        gather("v", k % 4, ids[t - 1][:, at(hd * TOPK + k, 1)])
            pool.wait_ge(s["idx_ready"], 1)
            with loop(pool, 8, (staged, 20), (used["u"], 4), (used["v"], 16)) as i:
                for r in range(4):
                    gather("u", r, ixS[:, at(i * 4 + r, 1)])
                    for q in range(4):
                        gather("v", q, ids[3][:, at(i * 16 + (4 * r + q), 1)])
            with loop(pool, 8, (staged, 4), (used["v"], 4)) as i:
                for r in range(4):
                    gather("v", r, ixS[:, at(i * 4 + r, 1)])

        @block.tensor
        def _(pe):
            mm = nc.tensor.matmul
            pairs, lap = Count(), Count()
            acc, ada_, h_in, yfree = Count(), Count(), Count(), Count()
            pe.sem_inc(s["y_done"], 2)

            def turn(items):
                pe.wait_ge(s["pair_free"], pairs.step())
                for out, in_ in items:
                    last = nc.tensor.transpose(out, in_, ident[0:in_.shape[0], 0:in_.shape[0]])
                last.then_inc(s["pair_full"], 1)

            def pair():
                return PAIR[pairs.n % 2]

            def arrived(j):
                pe.wait_ge(ring_full[j], lap.value() * 16 + 16)

            def product(weights, src, blocks, halves=(0, 1)):
                for h in halves:
                    pe.wait_ge(s["acc_free"], acc.step())
                    for n, (w, k) in enumerate(zip(weights, blocks)):
                        last = mm(ACC[h][:, 0:HALF], w, src[:, k, HALF * h:HALF * h + HALF],
                                  start=n == 0, stop=n == len(blocks) - 1)
                    last.then_inc(s["product_done"], 1)

            def main16(j, src, halves=(0, 1)):
                if 0 in halves:
                    arrived(j)
                product([slab16[j][:, k, :] for k in range(16)], src, range(16), halves)

            def main8(j, src):
                arrived(j)
                for m in range(2):
                    product([slab8[j][:, k, 128 * m:128 * m + 128] for k in range(8)], src, range(8))

            def ada_turn():
                pe.wait_ge(s["ada_free"], ada_.step())
                return mm(ADA[:, 128:128 + C9], ada_rows, fold[:, 0:C9], start=True, stop=True)

            def ada(j):
                arrived(j)
                ada_turn()
                for k in range(KD):
                    q = k % 4
                    last = mm(ADA[32 * q:32 * q + C9, 0:128], cT[:, k, :], slab16[j][:, k, :],
                              start=k < 4, stop=k >= KD - 4)
                last.then_inc(s["product_done"], 1)

            pe.wait_ge(s["consts_in"], 16)
            pe.wait_ge(s["silu_done"], 1)
            X, Z = pair()
            turn([(X[:, C9 * k:C9 * k + C9], A[0:C9, c_rows + 128 * k:c_rows + 128 * k + 128]) for k in range(KD)])
            pe.wait_ge(s["vec_in"], 96)
            X, Z = pair()
            turn([(X[:, 0:MODS], A[0:MODS, vec_rows:vec_rows + 128]),
                  (Z[:, 0:56], A[0:56, vec_rows + 128:vec_rows + 256])])
            pe.wait_ge(s["col_ready"], 1)
            mm(ADA[:, 0:128], ada_rows, ada_rows, start=True, stop=True)
            with loop(pe, 2, (lap, 1), (ada_, 4)):
                for j in range(4):
                    ada(j)
                lap.step()
            pe.wait_ge(s["rows_laid"], 1)
            X, Z = pair()
            turn([(X[:, 32 * k:32 * k + 32], A[0:32, par_rows + 128 * k:par_rows + 128 * k + 128])
                  for k in range(3)])
            pe.wait_ge(s["h0_in"], 64)
            X, Z = pair()
            turn([((X, Z)[k][:, 128 * u:128 * u + 128], h0_rows[k][:, u, :]) for k in range(2) for u in range(2)])
            with loop(pe, 3, (lap, 1), (ada_, 4)):
                for j in range(4):
                    ada(j)
                lap.step()
            pe.wait_ge(s["c_weights_in"], 16 * 16)
            for k in range(2):
                X, Z = pair()
                turn([((X, Z)[a // 4][:, 128 * (a % 4):128 * (a % 4) + 128], c_wide[k][:, a, :]) for a in range(NA)])
            pe.wait_ge(s["bb_ready"], 1)
            for k in range(2):
                X, Z = pair()
                turn([((X, Z)[a // 4][:, 128 * (a % 4):128 * (a % 4) + 128],
                       b_wide[k][:, 4 * a:4 * a + 4, :].rearrange("p a b -> p (a b)")) for a in range(NA)])
            with loop(pe, 3, (lap, 1), (ada_, 4)):
                for j in range(4):
                    ada(j)
                lap.step()
            ada_turn().then_inc(s["product_done"], 1)

            def rows_to_columns(src):
                for k in range(KD):
                    X, Z = pair()
                    turn([(X[:, 128 * t:128 * t + 128] if t < 4 else Z[:, 0:128],
                           src[:, t, 128 * k:128 * k + 128]) for t in range(ROWT)])

            def columns_to_rows(src, wide):
                for k in range(KD):
                    X, Z = pair()
                    turn([(X[:, 128 * t:128 * t + 128], src[:, k, 128 * t:128 * t + 128]) for t in range(4)]
                         + [(Z[:, 0:128], wide[:, k, :])])

            pe.wait_ge(s["xn_ready"], 1)
            rows_to_columns(x1)
            pe.wait_ge(s["col_ready"], 2)
            for _ in range(2):
                with loop(pe, 4, (lap, 1), (acc, 4), (ada_, 2)):
                    for j in (0, 2):
                        main16(j, hT)
                        ada(j + 1)
                    lap.step()

            def s5_in(b, n):
                X, Z = pair()
                pe.wait_ge(s["pair_free"], pairs.step())
                for k, out in enumerate((X, Z)):
                    for a in range(NA):
                        last = mm(out[:, n * a:n * a + n], BBT[k][32 * b:32 * b + 32, a, :],
                                  ustage[32 * b:32 * b + 32, a, 0:n], start=True, stop=True)
                last.then_inc(s["pair_full"], 1)

            def s5_out(b, n):
                pe.wait_ge(s["h_ready"], h_in.step())
                if b == 0:
                    pe.wait_ge(s["y_free"], yfree.step())
                hr, hi = HB[b % 2]
                for a in range(NA):
                    out = YB[32 * b:32 * b + 32, n * a:n * a + n]
                    mm(out, CTT[0][:, a, 32 * b:32 * b + 32], hr[:, n * a:n * a + n], start=True, stop=False)
                    last = mm(out, CTT[1][:, a, 32 * b:32 * b + 32], hi[:, n * a:n * a + n], start=False, stop=True)
                last.then_inc(s["y_done"], 1)

            stages = Count()

            def chunk(after):
                for b in range(NB):
                    if b < NB - 1:
                        s5_in(b + 1, L)
                    else:
                        pe.wait_ge(s["staged"], stages.step())
                        s5_in(0, after)
                    main16(2 * (b // 2), hT, (b % 2,))
                    if b % 2:
                        ada(2 * (b // 2) + 1)
                    s5_out(b, L)
                lap.step()

            pe.wait_ge(s["staged"], stages.step())
            s5_in(0, L)
            with loop(pe, CHUNKS - 1, (lap, 1), (acc, 4), (ada_, 2), (pairs, 4), (h_in, 4), (yfree, 1), (stages, 1)):
                chunk(L)
            chunk(NS)
            for b in range(NB):
                if b < NB - 1:
                    s5_in(b + 1, NS)
                s5_out(b, NS)
            pe.wait_ge(s["rows_laid"], 2)
            X, Z = pair()
            turn([(X[0:32, 128 * k:128 * k + 128], V(PH + 3072 + 32 * k, 32)) for k in range(2)]
                 + [(Z[:, 128 * k:128 * k + 128], V(PH + 3136 + 128 * k, 128)) for k in range(4)])
            pe.wait_ge(s["ub_ready"], 1)
            for c0, n in ((T - BUF, BUF), (T, NS)):
                X, Z = pair()
                turn([((X, Z)[a // 4][0:n, 128 * (a % 4):128 * (a % 4) + 128], ubT[:, a, c0:c0 + n])
                      for a in range(NA)])
            pe.wait_ge(s["pool_in"], 16)
            X, Z = pair()
            turn([((X, Z)[a // 4][:, 120 * (a % 4):120 * (a % 4) + 120],
                   A[0:SEQS * BUF, E + 128 * a:E + 128 * a + 128]) for a in range(NA)])
            pe.wait_ge(s["z_ready"], 1)
            for j in range(4):
                main8(j, uaT)
            lap.step()
            pe.wait_ge(s["wpool_in"], 16)
            pe.wait_ge(s["pooled"], 1)
            for g in range(4):
                for m in range(2):
                    product([wpool[:, 2 * g + k, 128 * m:128 * m + 128] for k in range(2)], ubT,
                            (2 * g, 2 * g + 1))
            pe.wait_ge(s["yb_ready"], 1)
            with loop(pe, 4, (lap, 1), (acc, 8), (ada_, 2)):
                for j in (0, 2):
                    main8(j, ybT)
                    ada(j + 1)
                lap.step()
            pe.wait_ge(s["ya_ready"], 1)
            with loop(pe, 8, (lap, 1), (acc, 8), (ada_, 1)):
                main16(0, hT)
                ada(1)
                main16(2, hT)
                main8(3, yaT)
                lap.step()
            pe.wait_ge(s["merged_ready"], 1)
            with loop(pe, 8, (lap, 1), (acc, 4), (ada_, 2)):
                for j in (0, 2):
                    main16(j, mT)
                    ada(j + 1)
                lap.step()
            ada_turn().then_inc(s["product_done"], 1)
            pe.wait_ge(s["expand_ready"], 1)
            columns_to_rows(hT, V3(MG, KD, 128))
            pe.wait_ge(s["xn_ready"], 2)
            rows_to_columns(xn)
            pe.wait_ge(s["expand_ready"], 2)
            columns_to_rows(mT, V3(HT, KD, 128))
            pe.wait_ge(s["keys_in"], 16)
            for half in range(2):
                X, Z = pair()
                turn([((X, Z)[k // 4][:, 128 * (k % 4):128 * (k % 4) + 128], keys_nat[:, 8 * half + k, :])
                      for k in range(8)])
            pe.wait_ge(s["keys_laid"], 1)
            with loop(pe, 8, (lap, 1), (acc, 4), (pairs, 2)) as i:
                for j in range(2):
                    main16(j, mT)
                    X, Z = pair()
                    pe.wait_ge(s["pair_free"], pairs.step())
                    pe.wait_ge(s["acc_free"], acc.value() + 2)
                    for t in range(ROWT):
                        last = mm(X[:, 128 * t:128 * t + 128] if t < 4 else Z[:, 0:128],
                                  qT[j][:, 128 * t:128 * t + 128],
                                  V(KT, 2048)[:, at((i * 2 + j) * 128, 128)], start=True, stop=True)
                    last.then_inc(s["pair_full"], 1)
                lap.step()
            pe.wait_ge(s["expand_ready"], 3)
            for q, rows in ((0, 128), (1, 128), (0, NS), (1, NS)):
                X, Z = pair()
                off = HT + (0 if rows == 128 else 2048)
                turn([((X, Z)[k // 4][0:rows, 128 * (k % 4):128 * (k % 4) + 128],
                       V(off + rows * (8 * q + k), rows)) for k in range(8)])
            pe.wait_ge(s["pair_full"], pairs.value())
            pe.sem_inc(s["v_used"], 4)

            vlap, dg = Count(), Count()
            for t in range(ROWT):
                rows = 128 if t < 4 else NS
                acc4 = psum4[t % 2]
                pe.wait_ge(s["peer_free"], t + 1)

                def slots(first, last_):
                    for r in range(4):
                        pe.wait_ge(s["diag_ready"], dg.step())
                        pe.wait_ge(v_full[r], vlap.value() * 16 + 16)
                        for n in range(4):
                            last = mm(acc4[0:rows, 512 * n:512 * n + 512], diag[r][:, 0:rows],
                                      vbuf[r][:, 512 * n:512 * n + 512],
                                      start=first and r == 0, stop=last_ and r == 3)
                        last.then_inc(s["v_used"], 1)
                    vlap.step()

                slots(True, False)
                with loop(pe, (32 if t < 4 else 8) - 2, (vlap, 1), (dg, 4)):
                    slots(False, False)
                slots(False, True)

        @block.scalar
        def _(act):
            fn = nc.scalar.activation
            product, acc, adas, pairs = Count(), Count(2), Count(1), Count()
            from_dve, pieces = Count(), Count()
            own = Own(act, s["act_step"])
            act.sem_inc(s["acc_free"], 2)
            act.sem_inc(s["ada_free"], 1)

            def read(h, out, func, free=True, **kw):
                act.wait_ge(s["product_done"], product.step())
                fn(out, ACC[h][:, 0:HALF], func, **kw).then_inc(s["acc_free"], 1)
                acc.step()

            def ada(m, rows=True):
                act.wait_ge(s["product_done"], product.step())
                if rows:
                    fn(ada_rows, ADA[:, 0:128], ACT.Copy)
                fn(A[:, at(m * C9 + (MOD - C9), C9)], ADA[:, 128:128 + C9], ACT.Identity,
                   bias=A[:, at(m + (BT - 1), 1)]).then_inc(s["ada_free"], 1)
                adas.step()

            def block_of(base, m):
                return [A[:, at(base + m * N + HALF * h, HALF)] for h in range(2)]

            def done(name, k=1):
                act.wait_ge(s["acc_free"], acc.value())
                act.sem_inc(s[name], k)

            act.wait_ge(s["c_in"], 32)
            cr = A[0:C9, c_rows:c_rows + D]
            fn(cr, cr, ACT.Silu).then_inc(s["silu_done"], 1)
            act.wait_ge(s["mods_ready"], 1)
            with loop(act, 2, (product, 4), (adas, 4)) as i:
                for j in range(4):
                    ada(i * 4 + j)
            dt, lr, ph, phabs = (V(PH + 64 + 32 * j, 32) for j in range(4))
            act.wait_ge(s["dve_to_act"], from_dve.step())
            fn(dt, dt, ACT.Exp).then_inc(s["act_to_dve"], 1)
            act.wait_ge(s["dve_to_act"], from_dve.step())
            fn(lr, lr, ACT.Exp)
            fn(ph, ph, ACT.Sin)
            act.wait_ge(s["consts_in"], 16)
            fn(phabs, phabs, ACT.Sin, scale=-1.0, bias=half_pi).then_inc(s["act_to_dve"], 1)
            with loop(act, 4, (product, 4), (adas, 4)) as i:
                for j in range(4):
                    ada(i * 4 + (8 + j))
            act.wait_ge(s["dve_to_act"], from_dve.step())
            fn(rstd, rstd, ACT.Sqrt).then_inc(s["act_to_dve"], 1)
            with loop(act, 2, (product, 4), (adas, 4)) as i:
                for j in range(4):
                    ada(i * 4 + (24 + j))
            ada(GT1, rows=False)
            act.wait_ge(s["ada_free"], adas.value())
            act.sem_inc(s["mods_ready"], 1)
            for base, m0, name in ((UA, 0, "ua_ready"), (UB, 8, "ub_ready")):
                with loop(act, 4, (product, 6), (acc, 4), (adas, 2)) as i:
                    for j in range(2):
                        for h in range(2):
                            read(h, block_of(base, i * 2 + j)[h], ACT.Copy)
                        ada(i * 2 + (GT1 + m0 + j))
                done(name)
                if name == "ua_ready":
                    fn(ustage, uaT[:, :, 0:L], ACT.Copy).then_inc(s["staged"], 1)
            pairs.n = S5_PAIR

            def chunk(c, last):
                for b in range(NB):
                    read(b % 2, block_of(MG, c * 2 + b // 2)[b % 2], ACT.Sigmoid)
                    if b % 2:
                        ada(c * 2 + (SH2 + b // 2))
                    if b == 2:
                        act.wait_ge(s["pair_full"], pairs.step(4))
                        if last:
                            fn(ustage[:, :, 0:NS], uaT[:, :, T:N], ACT.Copy).then_inc(s["staged"], 1)
                        else:
                            src = V(UA, KW * N).rearrange("p (a n) -> p a n", a=KW)
                            fn(ustage, src[:, :, at(c * L + L, L)], ACT.Copy).then_inc(s["staged"], 1)

            with loop(act, CHUNKS - 1, (product, 6), (acc, 4), (adas, 2), (pairs, 4)) as c:
                chunk(c, False)
            chunk(CHUNKS - 1, True)
            act.wait_ge(s["y_ready"], 1)
            fn(V(UA, KW * N), V(UA, KW * N), ACT.Gelu).then_inc(s["z_ready"], 1)
            for m in range(KW):
                for h in range(2):
                    read(h, yaT[:, m, HALF * h:HALF * h + HALF], ACT.Sigmoid, bias=bgluT[:, m:m + 1])
            done("glu_ready")
            for m in range(KW):
                for h in range(2):
                    read(h, ybT[:, m, HALF * h:HALF * h + HALF], ACT.Copy, scale=pscaleT[:, m:m + 1])
            done("yb_ready")

            def piece_out(h):
                act.wait_ge(s["piece_done"], pieces.step())
                read(h, piece[h], ACT.Copy)

            with loop(act, 4, (product, 10), (acc, 8), (adas, 2), (pieces, 8)) as i:
                for j in range(2):
                    for _ in range(2):
                        for h in range(2):
                            piece_out(h)
                    ada(i * 2 + (SC2 + j))
            with loop(act, 8, (product, 9), (acc, 8), (adas, 1), (pieces, 4)) as i:
                act.wait_ge(s["piece_done"], pieces.value() + 2)
                for j in range(2):
                    for h in range(2):
                        read(h, sig[2 * j + h], ACT.Sigmoid)
                    if j == 0:
                        ada(i + (SC2 + 8))
                for _ in range(2):
                    for h in range(2):
                        piece_out(h)
            act.wait_ge(s["ada_free"], adas.value())
            with loop(act, 8, (product, 6), (acc, 4), (adas, 2)) as i:
                for j in range(2):
                    m = i * 2 + j
                    gate = A[:, at(m * C9 + (MOD + GT1 * C9), 1)]
                    read(0, A[:, at(m * N + HT, HALF)], ACT.Copy, scale=gate)
                    act.wait_ge(s["product_done"], product.step())
                    fn(A[:, at(m * N + (HT + HALF), T - HALF)], ACC[1][:, 0:T - HALF], ACT.Copy, scale=gate)
                    fn(A[:, at(m * N + (HT + T), NS)], ACC[1][:, T - HALF:HALF], ACT.Copy
                       ).then_inc(s["acc_free"], 1)
                    acc.step()
                    ada(m + GT2)
            ada(MODS, rows=False)
            act.wait_ge(s["ada_free"], adas.value())
            done("out_ready")
            act.wait_ge(s["x1_ready"], 1)
            for t in range(3):
                own.then(fn(V(MG + D, D), x1[:, t, :], ACT.Square, accum_out=ss[:, t:t + 1]))
            act.sem_inc(s["act_to_dve"], 1)
            act.wait_ge(s["dve_to_act"], from_dve.step())
            fn(rstd, rstd, ACT.Sqrt).then_inc(s["act_to_dve"], 1)
            pairs.n = WQ_PAIR - 1
            with loop(act, 8, (product, 4), (acc, 4), (pairs, 2)):
                for j in range(2):
                    act.wait_ge(s["pair_full"], pairs.value())
                    pairs.step()
                    read(0, qT[j % 2][:, 0:HALF], ACT.Copy)
                    act.wait_ge(s["product_done"], product.step())
                    fn(qT[j % 2][:, HALF:T], ACC[1][:, 0:T - HALF], ACT.Copy)
                    fn(qT[j % 2][:, T:640].rearrange("p (r n) -> p r n", r=4),
                       bc(ACC[1][:, T - HALF:HALF], 1, 4), ACT.Copy).then_inc(s["acc_free"], 1)
                    acc.step()
            vused = Count()

            for st in range(ROWT + 1):
                if st:
                    t, n = st - 1, (32 if st - 1 < 4 else 8)
                    w, rows, base = wts[t % 2], (128 if t < 4 else NS), (ident if t < 4 else fold)
                    act.wait_ge(s["w_ready"], t + 1)
                    with loop(act, n, (vused, 4)) as i:
                        for r in range(4):
                            act.wait_ge(s["v_used"], vused.step())
                            fn(diag[r][:, 0:rows], base, ACT.Copy, scale=w[:, at(i * 4 + r, 1)]
                               ).then_inc(s["diag_ready"], 1)
                if st < ROWT:
                    cols = 128 if st < 4 else 32
                    act.wait_ge(s["act_ready"], st + 1)
                    fn(expo[:, 0:cols], expo[:, 0:cols], ACT.Exp).then_inc(s["gelu_ready"], 1)
                    fn(wts[st % 2][:, 0:cols], acts[st % 2][:, 0:cols], ACT.Gelu).then_inc(s["gelu_ready"], 1)
                if st:
                    act.wait_ge(s["fin_in"], st)
                    fn(V(KT + 1153, 1), V(KT + 1152, 1), ACT.Sqrt).then_inc(s["fin_sum"], 1)

        @block.vector
        def _(dve):
            v = nc.vector
            tt, ts, cp = v.tensor_tensor, v.tensor_scalar, v.tensor_copy
            me = Own(dve, s["dve_step"])
            did, settle, then = me.did, me.settle, me.then
            pf = Own(dve, s["pair_free"], 2)
            full, acc = Count(), Count(2)
            dve.sem_inc(s["pair_free"], 2)
            dve.sem_inc(s["y_free"], 1)
            dve.sem_inc(s["piece_done"], 2)
            dve.sem_inc(s["u_used"], 4)
            from_act = Count()

            def take():
                X, Z = PAIR[full.n % 2]
                dve.wait_ge(s["pair_full"], full.step())
                return X, Z

            def signal(name):
                settle()
                pf.settle()
                dve.sem_inc(s[name], 1)

            def to_act():
                signal("dve_to_act")

            def act_back():
                dve.wait_ge(s["act_to_dve"], from_act.step())

            did(v.memset(ada_rows, 0.0))
            for k in range(2):
                did(v.memset(V(MG + 3328 + 1024 * k, 1024), 0.0))
                did(v.memset(V(MG + 6400 + 1024 * k, 1024), 0.0))
            signal("c_zeroed")
            X, _ = take()
            pf.did(cp(V(CS, KD * C9), X[:, 0:KD * C9]))
            signal("col_ready")
            X, Z = take()
            did(cp(V(BT, MODS), X[:, 0:MODS]))
            pf.did(cp(vecs, Z[:, 0:56]))
            signal("mods_ready")
            dve.wait_ge(s["s5par_in"], 48)
            did(cp(A[0:32, par_rows + 256:par_rows + 384].rearrange("p (g q) -> p g q", g=2),
                   bc(A[0:32, par_rows + 384:par_rows + 386], 2, ST)))
            signal("rows_laid")
            X, _ = take()
            are, aim, dt, lr, ph, phabs, q, t1, t2, t3, t4, fre, fim, den = (V(PH + 32 * j, 32) for j in range(14))
            for k, dst in enumerate((are, aim, dt)):
                last = cp(dst.rearrange("p (b a) -> p b a", b=NB),
                          X[:, 32 * k:32 * k + 32].rearrange("p (a b) -> p b a", b=NB))
                (did if k < 2 else pf.did)(last)
            X, Z = take()
            for k, (src, dst) in enumerate(((X, h0[0]), (Z, h0[1]))):
                for b in range(NB):
                    last = cp(dst[:, 64 * b:64 * b + 64].rearrange("p (a q) -> p q a", a=NA),
                              src[:, 0:256].rearrange("p (q a b) -> p b q a", q=SEQS, a=NA)[:, b])
                    (pf.did if k == 1 and b == 3 else did)(last)
            to_act()
            act_back()
            did(tt(lr, are, dt, ALU.mult))
            then(tt(t1, aim, dt, ALU.mult))
            then(ts(q, t1, 1.0 / (2.0 * math.pi), None, ALU.mult))
            then(ts(q, q, ROUND, None, ALU.add))
            then(ts(q, q, -ROUND, None, ALU.add))
            for part in TWO_PI:
                then(v.scalar_tensor_tensor(out=t1, in0=q, scalar=-part, in1=t1, op0=ALU.mult, op1=ALU.add))
            then(ts(ph, t1, 3.1415925, -3.1415925, ALU.min, ALU.max))
            then(ts(t2, ph, -1.0, None, ALU.mult))
            did(tt(phabs, ph, t2, ALU.max))
            to_act()
            act_back()
            did(tt(abr, lr, phabs, ALU.mult))
            did(tt(abi, lr, ph, ALU.mult))
            did(tt(t1, are, are, ALU.mult))
            did(tt(t2, aim, aim, ALU.mult))
            settle()
            then(tt(den, t1, t2, ALU.add))
            did(v.reciprocal(den, den))
            did(ts(q, abr, -1.0, None, ALU.add))
            settle()
            did(tt(t1, q, are, ALU.mult))
            did(tt(t2, abi, aim, ALU.mult))
            did(tt(t3, abi, are, ALU.mult))
            did(tt(t4, q, aim, ALU.mult))
            settle()
            did(tt(fre, t1, t2, ALU.add))
            did(tt(fim, t3, t4, ALU.subtract))
            settle()
            did(tt(fre, fre, den, ALU.mult))
            did(tt(fim, fim, den, ALU.mult))
            settle()
            dve.wait_ge(s["b_weights_in"], 32)
            byba = "p (a b) c -> p b a c"
            for k in range(2):
                m1, m2 = V(PH + 512, 512), V(PH + 1024, 512)
                for g in range(2):
                    r = slice(64 * g, 64 * g + 64)
                    for b in range(NB):
                        for f, src, dst in ((fre, b_nat[k], m1), (fim, b_nat[1 - k], m2)):
                            did(tt(dst[r, 128 * b:128 * b + 128].rearrange("p (a c) -> p a c", a=NA),
                                   src[r].rearrange(byba, b=NB)[:, b], bc(f[r, 8 * b:8 * b + 8], 2, GC), ALU.mult))
                settle()
                for g in range(2):
                    r = slice(64 * g, 64 * g + 64)
                    for b in range(NB):
                        did(tt(b_wide[k][r].rearrange(byba, b=NB)[:, b, :, 16 * g:16 * g + 16],
                               m1[r, 128 * b:128 * b + 128].rearrange("p (a c) -> p a c", a=NA),
                               m2[r, 128 * b:128 * b + 128].rearrange("p (a c) -> p a c", a=NA),
                               ALU.subtract if k == 0 else ALU.add))
                settle()
            signal("bb_ready")
            for k in range(2):
                X, Z = take()
                did(ts(V(CT + 1024 * k, 512), X, (1.0, -1.0)[k], None, ALU.mult))
                pf.did(ts(V(CT + 1024 * k + 512, 512), Z, (1.0, -1.0)[k], None, ALU.mult))
            for k in range(2):
                X, Z = take()
                did(cp(V(BB + 1024 * k, 512), X))
                pf.did(cp(V(BB + 1024 * k + 512, 512), Z))

            def squares(tiles, junk):
                for t in tiles:
                    then(v.scalar_tensor_tensor(out=junk, in0=x1[:, t, :], scalar=1.0, in1=x1[:, t, :],
                                                op0=ALU.mult, op1=ALU.mult, accum_out=ss[:, t:t + 1]))

            def normalise(src, dst):
                then(ts(ss, ss, 1.0 / D, EPS, ALU.mult, ALU.add))
                did(v.reciprocal(rstd, ss))
                to_act()
                act_back()
                for t in range(ROWT):
                    did(ts(dst[:, t, :], src[:, t, :], rstd[:, t:t + 1], None, ALU.mult))
                signal("xn_ready")

            dve.wait_ge(s["x_in"], 80)
            squares(range(ROWT), V(HT, D))
            normalise(x1, x1)
            def modulate(base, dst, gain, sc, sh):
                g = mod[:, sc:sc + KD, :]
                then(v.scalar_tensor_tensor(out=g, in0=g, scalar=1.0, in1=bc(gain, 2, C9),
                                            op0=ALU.add, op1=ALU.mult))
                with loop(dve, 8, (full, 2), (pf.count, 2), (me.count, 2)) as i:
                    for j in range(2):
                        k = i * 2 + j
                        X, Z = take()
                        did(ts(A[:, at(k * N + base, T)], X, A[:, at(k * C9 + (MOD + sc * C9), 1)],
                               A[:, at(k * C9 + (MOD + sh * C9), 1)], ALU.mult, ALU.add))
                        pf.did(cp(A[:, at(k * N + (base + T), NS)], Z[:, 0:NS]))
                settle()
                pf.settle()
                seq = dst[:, :, T:N].rearrange("p k (q t) -> p k q t", q=SEQS)
                then(tt(seq, seq, bc(mod[:, sc:sc + KD, 1:C9], 3, STEPS), ALU.mult))
                then(tt(seq, seq, bc(mod[:, sh:sh + KD, 1:C9], 3, STEPS), ALU.add))

            dve.wait_ge(s["mods_ready"], 2)
            modulate(HT, hT, g1T, SC1, SH1)
            signal("col_ready")

            assert full.n == S5_PAIR
            pw = [V(PH + 448 + 32 * j, 32) for j in range(6)]
            cs_, sn_ = V(PH + 64 + 96, 32), V(PH + 64 + 64, 32)
            tc, tsn = V3(E, 32, L), V3(E + 2048, 32, L)
            did(v.memset(tc[:, :, 0:1], 1.0))
            did(v.memset(tsn[:, :, 0:1], 0.0))
            did(cp(pw[0], cs_))
            did(cp(pw[1], sn_))
            settle()
            n = 1
            while n < L:
                w1, w2 = V3(PH + 1024, 32, n), V3(PH + 2048, 32, n)
                pr, pi = bc(pw[0], 2, n), bc(pw[1], 2, n)
                did(tt(w1, tc[:, :, 0:n], pr, ALU.mult))
                then(tt(w2, tsn[:, :, 0:n], pi, ALU.mult))
                did(tt(tc[:, :, n:2 * n], w1, w2, ALU.subtract))
                settle()
                did(tt(w1, tc[:, :, 0:n], pi, ALU.mult))
                then(tt(w2, tsn[:, :, 0:n], pr, ALU.mult))
                did(tt(tsn[:, :, n:2 * n], w1, w2, ALU.add))
                did(tt(pw[2], pw[0], pw[0], ALU.mult))
                did(tt(pw[3], pw[1], pw[1], ALU.mult))
                did(tt(pw[4], pw[0], pw[1], ALU.mult))
                settle()
                did(tt(pw[0], pw[2], pw[3], ALU.subtract))
                did(ts(pw[1], pw[4], 2.0, None, ALU.mult))
                settle()
                n *= 2
            did(cp(V3(E + 4096, 32, L), bc(lr, 2, L)))
            did(cp(V3(E + 6144, 32, NS), bc(lr, 2, NS)))
            did(v.memset(V(HL, 64), 0.0))
            settle()
            did(v.memset(V3(E + 4096, 32, L)[:, :, 0:1], 0.0))
            did(v.memset(V3(E + 6144, 32 * SEQS, STEPS)[:, :, 0:1], 0.0))
            settle()

            ydone = Count()

            def carry(hr, hi, cr, ci, w, br, bi):
                did(tt(w[0], br, hr, ALU.mult))
                did(tt(w[1], bi, hi, ALU.mult))
                did(tt(w[2], br, hi, ALU.mult))
                did(tt(w[3], bi, hr, ALU.mult))
                settle()
                did(tt(cr, w[0], w[1], ALU.subtract))
                did(tt(ci, w[2], w[3], ALU.add))
                settle()

            def unit(b, sz, view, cos, sin, cf, cr, ci, first, save):
                X, Z = take()
                br, bi = X[:, 0:sz], Z[:, 0:sz]
                w1, w2, w3, w4 = (w[:, 0:sz] for w in (W1, W2, W3, W4))
                hr, hi = (w[:, 0:sz] for w in HB[b % 2])
                did(tt(view(w1), view(br), cos, ALU.mult))
                did(tt(view(w2), view(bi), sin, ALU.mult))
                did(tt(view(w3), view(bi), cos, ALU.mult))
                pf.did(tt(view(w4), view(br), sin, ALU.mult))
                settle()
                pf.settle()
                did(tt(w1, w1, w2, ALU.add))
                did(tt(w3, w3, w4, ALU.subtract))
                settle()
                did(tt(first(w1), first(w1), cr, ALU.add))
                did(tt(first(w3), first(w3), ci, ALU.add))
                settle()
                did(v.tensor_tensor_scan(w2, cf, w1, 0.0, ALU.mult, ALU.add))
                did(v.tensor_tensor_scan(w4, cf, w3, 0.0, ALU.mult, ALU.add))
                settle()
                dve.wait_ge(s["y_done"], ydone.step())
                did(tt(view(w1), view(w2), cos, ALU.mult))
                did(tt(view(w3), view(w4), sin, ALU.mult))
                did(tt(view(hi), view(w4), cos, ALU.mult))
                settle()
                did(tt(hr, w1, w3, ALU.subtract))
                did(tt(view(w4), view(w2), sin, ALU.mult))
                settle()
                did(tt(hi, hi, w4, ALU.add))
                settle()
                did(cp(save[0], save[2](hr)))
                did(cp(save[1], save[2](hi)))
                dve.sem_inc(s["h_ready"], 1)
                settle()

            def outputs(chunk_columns, n):
                did(tt(W1[:, 0:NA * n].rearrange("p (a n) -> p a n", a=NA), chunk_columns, bc(dT, 2, n), ALU.mult))
                settle()
                dve.wait_ge(s["y_done"], ylast.step(4))
                tt(chunk_columns, W1[:, 0:NA * n].rearrange("p (a n) -> p a n", a=NA),
                   YB[:, 0:NA * n].rearrange("p (a n) -> p a n", a=NA), ALU.add).then_inc(s["y_free"], 1)
                dve.wait_ge(s["y_free"], yout.step())

            ylast, yout = Count(2), Count(1)

            def chunk(before):
                carry(hlr, hli, crr, cri, [V(PH + 32 * j, 32) for j in range(4)], abr, abi)
                for b in range(NB):
                    col = slice(8 * b, 8 * b + 8)
                    unit(b, 512, lambda w: w, tabc[:, b].rearrange("p a t -> p (a t)"),
                         tabs[:, b].rearrange("p a t -> p (a t)"), coef[:, b].rearrange("p a t -> p (a t)"),
                         crr[:, col], cri[:, col],
                         lambda w: w.rearrange("p (a t) -> p a t", a=NA)[:, :, 0],
                         (hlr[:, col], hli[:, col],
                          lambda w: w.rearrange("p (a t) -> p a t", a=NA)[:, :, L - 1]))
                    if b == 0 and before is not None:
                        outputs(before, L)

            dve.wait_ge(s["ua_ready"], 1)
            chunk(None)
            with loop(dve, CHUNKS - 1, (me.count, 75), (pf.count, 4), (full, 4), (ydone, 4), (ylast, 4),
                      (yout, 1)) as c:
                chunk(uaT[:, :, at(c * L, L)])
            abrS, abiS = bc(abr, 2, SEQS), bc(abi, 2, SEQS)

            def by_state(w):
                return w.rearrange("p (i q) -> p i q", q=SEQS)

            cS = (V(PH + 1280, 256), V(PH + 1792, 256))
            carry(by_state(h0[0]), by_state(h0[1]), by_state(cS[0]), by_state(cS[1]),
                  [by_state(V(PH + 256 * j, 256)) for j in range(4)], abrS, abiS)
            for b in range(NB):
                col = slice(64 * b, 64 * b + 64)
                unit(b, 256, lambda w: w.rearrange("p (a q t) -> p a q t", a=NA, q=SEQS),
                     bc(tabc[:, b, :, 0:STEPS], 2, SEQS), bc(tabs[:, b, :, 0:STEPS], 2, SEQS),
                     coefS[:, 256 * b:256 * b + 256], cS[0][:, col], cS[1][:, col],
                     lambda w: w.rearrange("p (i t) -> p i t", t=STEPS)[:, :, 0],
                     (h0[0][:, col], h0[1][:, col],
                      lambda w: w.rearrange("p (i t) -> p i t", t=STEPS)[:, :, STEPS - 1]))
                if b == 0:
                    outputs(uaT[:, :, T - L:T], L)
            outputs(uaT[:, :, T:N], NS)
            dve.wait_ge(s["y_free"], yout.value())
            dve.sem_inc(s["y_ready"], 1)
            signal("s5_done")
            for k, src in enumerate((hlr, hli)):
                did(cp(V(PH + 3072 + 32 * k, 32).rearrange("p (a b) -> p b a", b=NB),
                       src.rearrange("p (b a) -> p b a", b=NB)))
            for k in range(2):
                for b in range(NB):
                    did(cp(V(PH + 3136 + 256 * k, 256).rearrange("p (q a b) -> p b a q", q=SEQS, a=NA)[:, b],
                           h0[k][:, 64 * b:64 * b + 64].rearrange("p (a q) -> p a q", a=NA)))
            signal("rows_laid")
            X, Z = take()
            did(cp(A[0:32, PH:PH + 256], X[0:32, 0:256]))
            pf.did(cp(V(PH + 256, 512), Z))
            for rows, dst in ((BUF, out_prompt_rows), (NS, out_sample_rows)):
                X, Z = take()
                did(cp(dst[0:rows, 0:512], X[0:rows, :]))
                pf.did(cp(dst[0:rows, 512:1024], Z[0:rows, :]))
            signal("state_rows")
            dve.wait_ge(s["state_out"], 256)
            PA, PB = V3(PH, 2, T + BUF), V3(PH + 1054, 2, T + BUF)
            for g, win in enumerate(WINDOWS):
                u = ubT[:, 2 * g:2 * g + 2, 0:T]
                did(v.memset(PA[:, :, 0:BUF], 0.0))
                did(cp(PA[:, :, BUF:], u))
                settle()
                src, dst = PA, PB
                for lev in range(g + 1):
                    lo, sh = 2 ** (lev + 1) - 1, 2 ** lev
                    then(tt(dst[:, :, lo:], src[:, :, lo:], src[:, :, lo - sh:T + BUF - sh], ALU.add))
                    src, dst = dst, src
                then(tt(src[:, :, BUF:BUF + 16], src[:, :, BUF:BUF + 16], bc(corr[:, g, :], 1, 2), ALU.mult))
                then(v.scalar_tensor_tensor(out=u, in0=src[:, :, BUF:], scalar=1.0 / win, in1=u,
                                            op0=ALU.mult, op1=ALU.subtract))
            EX = V(PH + 2108, 1216).rearrange("p (a q e) -> p a q e", a=KW, q=SEQS)
            EB = [V(PH + 3324 + 304 * j, 304).rearrange("p (a q e) -> p a q e", a=2, q=SEQS) for j in range(2)]
            X, Z = take()
            for k, src in enumerate((X, Z)):
                last = cp(EX[:, 4 * k:4 * k + 4, :, 0:BUF],
                          src[:, 0:480].rearrange("p (a q e) -> p a q e", a=4, q=SEQS))
                (did if k == 0 else pf.did)(last)
            for a in range(KW):
                did(cp(EX[:, a, :, BUF:], ubT[:, a, T:N].rearrange("p (q t) -> p q t", q=SEQS)))
            settle()
            pf.settle()
            for g, win in enumerate(WINDOWS):
                src, dst = EX[:, 2 * g:2 * g + 2], EB[0]
                for lev in range(g + 1):
                    lo, sh = 2 ** (lev + 1) - 1, 2 ** lev
                    then(tt(dst[:, :, :, lo:], src[:, :, :, lo:], src[:, :, :, lo - sh:19 - sh], ALU.add))
                    src, dst = dst, EB[(lev + 1) % 2]
                then(ts(src[:, :, :, BUF:], src[:, :, :, BUF:], 1.0 / win, None, ALU.mult))
                for a in range(2):
                    u = ubT[:, 2 * g + a, T:N].rearrange("p (q t) -> p q t", q=SEQS)
                    did(tt(u, src[:, a, :, BUF:], u, ALU.subtract))
                settle()
            signal("pooled")
            dve.wait_ge(s["glu_ready"], 1)
            then(tt(V(BB, KW * N), V(BB, KW * N), V(UA, KW * N), ALU.mult))
            signal("ya_ready")

            acc.n = 2 + 2 * (8 + 8 + 16 + 8 + 8)

            def gated(m, h, gate=None):
                dst = A[:, at(m * N + (MG + HALF * h), HALF)]
                if gate is None:
                    dve.wait_ge(s["acc_free"], acc.step())
                    tt(dst, dst, piece[h], ALU.mult).then_inc(s["piece_done"], 1)
                else:
                    then(tt(piece[h], piece[h], gate, ALU.mult))
                    tt(dst, dst, piece[h], ALU.add).then_inc(s["piece_done"], 1)

            with loop(dve, 4, (acc, 8)) as i:
                for m in range(4):
                    for h in range(2):
                        gated(i * 4 + m, h)
            with loop(dve, 8, (acc, 8), (me.count, 4)) as i:
                acc.step(4)
                for m in range(2):
                    for h in range(2):
                        dve.wait_ge(s["acc_free"], acc.step())
                        gated(i * 2 + m, h, sig[2 * m + h])
            dve.wait_ge(s["piece_done"], 2 + 64)
            signal("merged_ready")

            dve.wait_ge(s["out_ready"], 1)
            seq = hT[:, :, T:N].rearrange("p k (q t) -> p k q t", q=SEQS)
            then(tt(seq, seq, bc(mod[:, GT1:GT1 + KD, 1:C9], 3, STEPS), ALU.mult))
            did(cp(V(MG, D).rearrange("p (k r n) -> p k r n", k=KD, r=4), bc(hT[:, :, T:N], 2, 4)))
            signal("expand_ready")
            dve.wait_ge(s["x_in"], 160)

            def rows_from_pairs(dst, op):
                with loop(dve, 8, (full, 2), (pf.count, 2), (me.count, 2)) as i:
                    for j in range(2):
                        X, Z = take()
                        x4 = dst[:, 0:4, at((i * 2 + j) * 128, 128)]
                        xs = dst[:, 4, at((i * 2 + j) * 128, 128)]
                        X4 = X.rearrange("p (t n) -> p t n", t=4)
                        if op:
                            did(tt(x4, x4, X4, ALU.add))
                            pf.did(tt(xs, xs, Z[:, 0:128], ALU.add))
                        else:
                            did(cp(x4, X4))
                            pf.did(cp(xs, Z[:, 0:128]))

            rows_from_pairs(x1, True)
            signal("x1_ready")
            squares((3, 4), V(MG + 2 * D, D))
            act_back()
            normalise(x1, xn)
            modulate(MG, mT, g2T, SC2, SH2)
            did(cp(V(HT, D).rearrange("p (k r n) -> p k r n", k=KD, r=4), bc(mT[:, :, T:N], 2, 4)))
            signal("expand_ready")
            rows_from_pairs(xn, False)
            for half in range(2):
                X, Z = take()
                did(cp(V(KT + 1024 * half, 512), X))
                pf.did(cp(V(KT + 1024 * half + 512, 512), Z))
            signal("keys_laid")

            assert full.n == WQ_PAIR
            S2 = V3(HT + 1280, ROWT, 128)
            tsc = V4(HT + 1920, ROWT, 2, 16)
            tix = V4(HT + 2080, ROWT, 2, 16).bitcast(U32)

            filled = [Count() for _ in range(4)]

            def dot(r, t, column, early=False):
                row = (ubuf1 if early else ubuf)[r]
                dve.wait_ge(u_full[r], filled[r].step(16))
                v.scalar_tensor_tensor(out=row, in0=row, scalar=1.0, in1=xn[:, t, :],
                                       op0=ALU.mult, op1=ALU.mult, accum_out=acts[t % 2][:, column]
                                       ).then_inc(s["u_used"], 1)

            def top16(src, spare, score, index, dots):
                def stand():
                    settle()
                    dve.sem_inc(s["dve_stood"], 1)

                stand()
                for t in range(len(src)):
                    did(v.max(score[t][:, 0:8], src[t]))
                stand()
                for t in range(len(src)):
                    did(v.max_index(index[t][:, 0:8], score[t][:, 0:8], src[t]))
                    did(v.match_replace(spare[t], score[t][:, 0:8], src[t], LOW))
                dots()
                stand()
                for t in range(len(src)):
                    did(v.max(score[t][:, 8:16], spare[t]))
                dots()
                stand()
                for t in range(len(src)):
                    did(v.max_index(index[t][:, 8:16], score[t][:, 8:16], spare[t]))
                dots()
                stand()

            class Dots:

                def __init__(self, tile, head, early=False):
                    self.tile, self.head, self.early, self.k = tile, head, early, 0

                def __call__(self, k=1):
                    for _ in range(min(k, TOPK - self.k)):
                        dot(self.k % 4, self.tile, at(self.head * TOPK + self.k, 1), self.early)
                        self.k += 1

            def choose(tile, hd, scores, places, work, dots):
                comb, rest, hot = V(work, SUMS), V(work + 112, SUMS), V3(work + 224, 16, 16)
                part_i, part_f = V(work + 480, 64).bitcast(U32), V(work + 544, 64)
                place = [V(work + 608 + 16 * j, 16) for j in range(2)]
                sc, bj = V(work + 640, 16), V(work + 656, 16).bitcast(U32)
                did(tt(comb[:, 0:64].rearrange("p (a b) -> p a b", a=4),
                       bc(scores[:, 0, 0:4], 2, 16), bc(scores[:, 1, :], 1, 4), ALU.add))
                did(tt(comb[:, 64:SUMS].rearrange("p (a b) -> p a b", a=12),
                       bc(scores[:, 0, 4:16], 2, 4), bc(scores[:, 1, 0:4], 1, 12), ALU.add))
                dots()
                top16([comb], [rest], [sc], [bj], dots)
                did(cp(best[tile][:, at(hd * TOPK, TOPK)], sc))
                for k, (op, by) in enumerate(((ALU.logical_shift_right, 4), (ALU.bitwise_and, 15),
                                              (ALU.logical_shift_right, 2), (ALU.bitwise_and, 3))):
                    did(ts(part_i[:, 16 * k:16 * k + 16], bj, by, None, op))
                dots()
                settle()
                then(cp(part_f, part_i))
                low, high = part_f[:, 0:32], part_f[:, 32:64]
                then(ts(high[:, 0:16], high[:, 0:16], -12.0, None, ALU.add))
                did(ts(place[0], high[:, 0:16], 4.0, None, ALU.is_ge))
                dots()
                settle()
                then(tt(high, high, low, ALU.subtract))
                high3 = high.rearrange("p (k n) -> p k n", k=2)
                then(tt(high3, high3, bc(place[0], 1, 2), ALU.mult))
                then(tt(low, low, high, ALU.add))
                for k in range(2):
                    dots()
                    then(tt(hot, bc(low[:, 16 * k:16 * k + 16], 2, 16), bc(iota16, 1, 16), ALU.is_equal))
                    then(tt(hot, hot, bc(places[:, k, :], 1, 16), ALU.mult))
                    dots()
                    then(v.tensor_reduce(place[k], hot, AX.X, ALU.add))
                then(v.scalar_tensor_tensor(out=ids[tile][:, at(hd * TOPK, TOPK)], in0=place[0], scalar=128.0,
                                            in1=place[1], op0=ALU.mult, op1=ALU.add))

            def choose_later(tile, hd, dots):
                cur = [V(PICK + 672 + 32 * j, 32) for j in range(2)]
                did(cp(cur[0], V(BEST + 256 * tile, 256)[:, at(hd * 32, 32)]))
                did(cp(cur[1], V(ID[tile], 256)[:, at(hd * 32, 32)]))
                settle()
                choose(tile, hd, *(c.rearrange("p (h k) -> p h k", h=2) for c in cur), PICK, dots)

            def head(hd, dots):
                for half in range(2):
                    X, Z = take()
                    src = [X[:, 128 * t:128 * t + 128] for t in range(4)] + [Z[:, 0:128]]
                    top16(src, [S2[:, t, :] for t in range(ROWT)], [tsc[:, t, half, :] for t in range(ROWT)],
                          [tix[:, t, half, :] for t in range(ROWT)], dots)
                    dve.sem_inc(s["pair_free"], 1)
                    pf.count.step()
                did(cp(V3(BEST + 256, 4, 256)[:, :, at(hd * 32, 32)], tsc[:, 1:5].rearrange("p t h k -> p t (h k)")))
                for first, n in ((1, 2), (3, 2)):
                    did(cp(V3(ID[first], n, 256)[:, :, at(hd * 32, 32)],
                           tix[:, first:first + n].rearrange("p t h k -> p t (h k)")))
                tif = V3(HT + 2240, 2, 16)
                then(cp(tif, tix[:, 0]))
                choose(0, hd, tsc[:, 0], tif, HT + 2304, dots)
                dots(TOPK)
                dve.sem_inc(s["head_ready"], 1)

            head(0, lambda k=1: None)
            with loop(dve, HEADS - 1, (full, 2), (pf.count, 2), (me.count, 79),
                      *((c, 64) for c in filled)) as hd:
                head(hd + 1, Dots(0, hd, early=True))
            did(cp(V(HT, D).rearrange("p (k n) -> p k n", k=KD), bc(mod[:, GT2:GT2 + KD, 0], 2, 128)))
            for q in range(SEQS):
                did(cp(V3(HT + D, KD, NS)[:, :, STEPS * q:STEPS * q + STEPS],
                       bc(mod[:, GT2:GT2 + KD, 1 + q], 2, STEPS)))
            signal("expand_ready")
            dots = Dots(0, HEADS - 1)
            dots(4)
            for dst, rows in ((gt2P, 128), (gt2S, NS)):
                for q in range(2):
                    X, Z = take()
                    did(cp(dst[0:rows, 1024 * q:1024 * q + 512], X[0:rows, :]))
                    pf.did(cp(dst[0:rows, 1024 * q + 512:1024 * q + 1024], Z[0:rows, :]))
            pf.settle()
            dve.sem_inc(s["peer_free"], 2)

            ms, root = V(KT + 1152, 1), V(KT + 1153, 1)
            done_v = 4
            for st in range(ROWT + 1):
                if st in (1, 2, 3):
                    per = 27 * (1 if st < 3 else 2)
                    with loop(dve, HEADS - 1, (me.count, per), *((c, 64) for c in filled)) as hd:
                        dots = Dots(st, hd)
                        choose_later(st, hd + 1, dots)
                        dve.sem_inc(s["head_ready"], 1)
                        if st == 3:
                            choose_later(4, hd + 1, dots)
                        dots(TOPK)
                    dots = Dots(st, HEADS - 1)
                if st < 3:
                    choose_later(st + 1, 0, dots)
                    dve.sem_inc(s["head_ready"], 1)
                    if st == 2:
                        choose_later(4, 0, dots)
                if st == 3:
                    for r in range(4):
                        p4 = slice(32 * r, 32 * r + 32)
                        did(cp(ixS[p4], ids[4][p4, 32 * r:32 * r + 32]))
                        did(cp(gS[p4], best[4][p4, 32 * r:32 * r + 32]))
                    settle()
                    dve.sem_inc(s["idx_ready"], 1)
                if st < 4:
                    dots(TOPK)
                if st == 4:
                    with loop(dve, 8, *((c, 16) for c in filled)) as i:
                        for r in range(4):
                            dot(r, st, at(i * 4 + r, 1))
                if st < ROWT:
                    n = SLOTS if st < 4 else SLOTS // 4
                    chosen = (best[st] if st < 4 else gS).rearrange("p (h k) -> p h k", k=TOPK)
                    ex, w = expo[:, 0:n].rearrange("p (h k) -> p h k", k=TOPK), wts[st % 2][:, 0:n]
                    w3, total = w.rearrange("p (h k) -> p h k", k=TOPK), sums[:, 0:n // TOPK]
                    then(tt(ex, chosen, bc(chosen[:, :, 0], 2, TOPK), ALU.subtract))
                    dve.wait_ge(s["u_used"], 4 + (128 * (st + 1) if st < 4 else 512 + 32))
                    dve.sem_inc(s["act_ready"], 1)
                    dve.wait_ge(s["gelu_ready"], 2 * st + 2)
                    did(v.tensor_reduce(total, ex, AX.X, ALU.add))
                    did(tt(w3, w3, ex, ALU.mult))
                    settle()
                    then(v.reciprocal(total, total))
                    did(tt(w3, w3, bc(total, 2, TOPK), ALU.mult))
                    signal("w_ready")
                if st:
                    t = st - 1
                    rows, gt2 = (128, gt2P) if t < 4 else (NS, gt2S)
                    done_v += 128 if t < 4 else 32
                    dve.wait_ge(s["v_used"], done_v)
                    if t == 0:
                        dve.wait_ge(s["gfinal_in"], 16)
                    f, x = fin[0:rows], x1[0:rows, t, :]
                    then(tt(f, psum4[t % 2][0:rows, :], gt2[0:rows], ALU.mult))
                    dve.sem_inc(s["peer_free"], 1)
                    then(tt(x, x, f, ALU.add))
                    then(v.scalar_tensor_tensor(out=f, in0=x, scalar=1.0, in1=x, op0=ALU.mult, op1=ALU.mult,
                                                accum_out=ms[0:rows]))
                    then(ts(ms[0:rows], ms[0:rows], 1.0 / D, EPS, ALU.mult, ALU.add))
                    then(v.reciprocal(ms[0:rows], ms[0:rows]))
                    dve.sem_inc(s["fin_in"], 1)
                    dve.wait_ge(s["fin_sum"], t + 1)
                    then(v.scalar_tensor_tensor(out=x, in0=x, scalar=root[0:rows], in1=gfin[0:rows],
                                                op0=ALU.mult, op1=ALU.mult))
                    dve.sem_inc(s["fin_row"], 1)


INPUTS = {
    "x_prompt": None, "x_sample": None, "state_s5_re": (SEQS, G, ST), "state_s5_im": (SEQS, G, ST),
    "state_pool": (SEQS, BUF, W), "c_prompt": None, "c_sample": None, "w_ada": (D, 6 * D), "b_ada": (6 * D,),
    "g_norm1": (D,), "g_norm2": (D,), "w_in": (D, 3 * D), "s5_a_re": (G, ST), "s5_a_im": (G, ST),
    "s5_log_dt": (G,), "s5_b_re": (G, ST, GC), "s5_b_im": (G, ST, GC), "s5_c_re": (G, GC, ST),
    "s5_c_im": (G, GC, ST), "s5_d": (W,), "w_glu": (W, W), "b_glu": (W,), "w_pool": (4, 256, 256),
    "pool_scale": (W,), "w_proj_a": (W, D), "w_proj_b": (W, D), "w_out": (D, D), "peer_wq": (D, D),
    "peer_keys": (HEADS, 2, 128, 128), "peer_u": (16384, D), "peer_v": (16384, D), "g_final": None,
}
OUTPUTS = {
    "y_prompt": (1, T, D), "y_sample": (SEQS, STEPS, D), "new_s5_re_prompt": (G, ST), "new_s5_im_prompt": (G, ST),
    "new_pool_prompt": (BUF, W), "new_s5_re_sample": (SEQS, G, ST), "new_s5_im_sample": (SEQS, G, ST),
    "new_pool_sample": (SEQS, BUF, W),
}
RETURNED = [(1, T, D), (SEQS, STEPS, D), (1, 1, G, ST), (1, 1, G, ST), (1, 1, BUF, W), (1, SEQS, G, ST),
            (1, SEQS, G, ST), (1, SEQS, BUF, W)]


def constants():
    c = np.zeros((P, NCON), np.float32)
    c[:, 0:128] = np.eye(P)
    c[:, 128:144] = np.arange(16)
    for g, w in enumerate(WINDOWS):
        c[:, 144 + 16 * g:160 + 16 * g] = w / np.minimum(np.arange(16) + 1, w)
    c[:, 208:240] = np.tile(np.eye(NS), (4, 1))
    c[:, 240] = math.pi / 2
    return c


def kernel(**inputs):
    import concourse.bacc as bacc
    from concourse.bass_utils import run_bass_kernel_spmd

    nc = bacc.Bacc("TRN2", target_bir_lowering=False, num_devices=1)
    arrays, ins, outs = {}, {}, {}
    for name, shape in INPUTS.items():
        a = np.ascontiguousarray(inputs[name])
        arrays[name] = a if shape is None else a.reshape(shape)
    arrays["consts"] = constants()
    for name, a in arrays.items():
        ins[name] = nc.dram_tensor(name, a.shape, F32, kind="ExternalInput").ap()
    for name, shape in OUTPUTS.items():
        outs[name] = nc.dram_tensor(name, shape, F32, kind="ExternalOutput").ap()
    layer(nc, ins, outs)
    r = run_bass_kernel_spmd(nc, [arrays], core_ids=[0]).results[0]
    return tuple(r[name].reshape(shape) for name, shape in zip(OUTPUTS, RETURNED))
```
